# Optimizing a Trainium2 kernel written in Bass

```python
import math
import jax
import jax.numpy as jnp
from jax import lax
import numpy as np

D_MODEL = 1024
BATCH = 1
SEQ = 128
DEPTH = 2
DEC_BATCH = 1
DEC_SEQ = 256
PAST_LEN = 128

GRID_W = 64
N_EVEN = (DEPTH + 1) // 2
N_ODD = DEPTH // 2
H_A = 4
DK_A = 128
DV_A = D_MODEL // 2 // H_A
F_A = H_A * DK_A
CHUNK = 64
H_B = 8
KV_B = 2
G_B = H_B // KV_B
HD_B = D_MODEL // 2 // H_B
WINDOW = 128
QBLK = 128
H_C = 8
HD_C = D_MODEL // (2 * H_C)
D_FF = 4 * D_MODEL
ROPE_BASE = 10000.0
EPS = 1e-6
D_MIX = D_MODEL
EVEN_SIZES = (F_A, F_A, F_A, H_A * DV_A, H_A * DV_A, H_B * HD_B, KV_B * HD_B, KV_B * HD_B)
EVEN_COLS = 3 * F_A + 2 * H_A * DV_A + (H_B + 2 * KV_B) * HD_B
ODD_W = H_C * 2 * HD_C
ODD_COLS = 3 * ODD_W

kernel_name = "hybrid_dit_hgrn2_swa_diffattn_step"

F32 = jnp.float32

def rms_norm(x, w):
    xf = x.astype(F32)
    y = xf * lax.rsqrt(jnp.mean(xf * xf, axis=-1, keepdims=True) + EPS)
    return (y * w.astype(F32)).astype(x.dtype)

def split_cols(a, sizes):
    out, start = [], 0
    for s in sizes:
        out.append(a[..., start:start + s])
        start += s
    return out

def ada_mods(cvec, w_ada, b_ada):
    m = jax.nn.silu(cvec) @ w_ada + b_ada
    return jnp.split(m[:, None, :], 6, axis=-1)

def rope_2d(x):
    L, d = x.shape[1], x.shape[-1]
    t = jnp.arange(L)
    row = (t // GRID_W).astype(F32)
    col = (t % GRID_W).astype(F32)
    half = d // 2
    inv = ROPE_BASE ** (-jnp.arange(0, half, 2, dtype=F32) / half)
    ang = jnp.concatenate([row[:, None] * inv, col[:, None] * inv], -1)[None, :, None, :]
    cos, sin = jnp.cos(ang), jnp.sin(ang)
    xf = x.astype(F32)
    x1, x2 = xf[..., 0::2], xf[..., 1::2]
    return jnp.stack([x1 * cos - x2 * sin, x1 * sin + x2 * cos], -1).reshape(x.shape).astype(x.dtype)

def map_query_blocks(fn, q):
    b, l = q.shape[:2]
    n = l // QBLK
    qb = jnp.moveaxis(q.reshape((b, n, QBLK) + q.shape[2:]), 1, 0)
    out = lax.map(lambda xs: fn(xs[0], xs[1]), (qb, jnp.arange(n)))
    return jnp.moveaxis(out, 0, 1).reshape((b, l) + out.shape[3:])

def hgrn_scan(q, k, v, g, s0):
    b, h, l, _ = q.shape
    n = l // CHUNK
    def chunks(a):
        return jnp.moveaxis(a.reshape(b, h, n, CHUNK, a.shape[-1]), 2, 0)
    tril = jnp.tril(jnp.ones((CHUNK, CHUNK), bool))[:, :, None]
    def step(s, xs):
        qc, kc, vc, gc = xs
        cum = jnp.cumsum(gc, axis=2)
        diff = cum[:, :, :, None, :] - cum[:, :, None, :, :]
        decay = jnp.exp(jnp.where(tril, diff, -jnp.inf))
        att = jnp.einsum('bhtk,bhsk,bhtsk->bhts', qc, kc, decay)
        o = jnp.einsum('bhts,bhsv->bhtv', att, vc) + jnp.einsum('bhtk,bhkv->bhtv', qc * jnp.exp(cum), s)
        last = cum[:, :, -1:, :]
        s_new = jnp.exp(last[:, :, 0, :])[..., None] * s + jnp.einsum('bhsk,bhsv->bhkv', kc * jnp.exp(last - cum), vc)
        return s_new, o
    s_fin, o = lax.scan(step, s0, (chunks(q), chunks(k), chunks(v), chunks(g)))
    return jnp.moveaxis(o, 0, 2).reshape(b, h, l, -1), s_fin

def hgrn_bidir(q, g_f, g_b, v, s_f0, s_b0):
    o_f, s_f = hgrn_scan(q, -jnp.expm1(g_f), v, g_f, s_f0)
    rev = lambda a: jnp.flip(a, axis=2)
    o_b, s_b = hgrn_scan(rev(q), rev(-jnp.expm1(g_b)), rev(v), rev(g_b), s_b0)
    return o_f + rev(o_b), jnp.stack([s_f, s_b], axis=1)

def hgrn_readout(o, gate, norm_w):
    o = rms_norm(o.transpose(0, 2, 1, 3), norm_w) * jax.nn.silu(gate.astype(F32))
    return o.reshape(o.shape[0], o.shape[1], -1).astype(gate.dtype)

def even_inputs(h, w_in, lb, qn_w, kn_w):
    b, l = h.shape[:2]
    qa, zf, zb, ia, ga, qb, kb, vb = split_cols(h @ w_in, EVEN_SIZES)
    def rec(a, d):
        return a.reshape(b, l, H_A, d).transpose(0, 2, 1, 3).astype(F32)
    q_r = rec(jax.nn.silu(qa), DK_A) * (DK_A ** -0.5)
    lbf = lb.astype(F32).reshape(2, H_A, 1, DK_A)
    g_f = jnp.log(lbf[0] + (1.0 - lbf[0]) * jax.nn.sigmoid(rec(zf, DK_A)))
    g_b = jnp.log(lbf[1] + (1.0 - lbf[1]) * jax.nn.sigmoid(rec(zb, DK_A)))
    v_r = rec(ia, DV_A)
    gate = ga.reshape(b, l, H_A, DV_A)
    q_a = rms_norm(qb.reshape(b, l, H_B, HD_B), qn_w)
    k_a = rms_norm(kb.reshape(b, l, KV_B, HD_B), kn_w)
    v_a = vb.reshape(b, l, KV_B, HD_B)
    return (q_r, g_f, g_b, v_r, gate), (q_a, k_a, v_a)

def swa_context_attention(q, k, v, sink):
    b, l = q.shape[:2]
    qg = q.reshape(b, l, KV_B, G_B, HD_B)
    sink_l = sink.astype(F32).reshape(KV_B, G_B, 1, 1)
    def blk(qb, _i):
        s = jnp.einsum('bqngd,bknd->bngqk', qb, k).astype(F32) * HD_B ** -0.5
        s = jnp.concatenate([s, jnp.broadcast_to(sink_l, s.shape[:-1] + (1,))], -1)
        pr = jax.nn.softmax(s, axis=-1)[..., :-1].astype(v.dtype)
        return jnp.einsum('bngqk,bknd->bqngd', pr, v)
    return map_query_blocks(blk, qg).reshape(b, l, H_B * HD_B)

def swa_latent_attention(q, k, v, k_ctx, v_ctx, sink):
    b, l = q.shape[:2]
    qg = q.reshape(b, l, KV_B, G_B, HD_B)
    pad = ((0, 0), (WINDOW, WINDOW), (0, 0), (0, 0))
    k_pad, v_pad = jnp.pad(k, pad), jnp.pad(v, pad)
    span = QBLK + 2 * WINDOW
    sink_l = sink.astype(F32).reshape(KV_B, G_B, 1, 1)
    def blk(qb, i):
        start = i * QBLK
        kw = lax.dynamic_slice_in_dim(k_pad, start, span, axis=1)
        vw = lax.dynamic_slice_in_dim(v_pad, start, span, axis=1)
        tq = start + jnp.arange(QBLK)
        tk = start - WINDOW + jnp.arange(span)
        valid = (jnp.abs(tq[:, None] - tk[None, :]) <= WINDOW) & (tk >= 0)[None, :] & (tk < l)[None, :]
        s_w = jnp.einsum('bqngd,bknd->bngqk', qb, kw).astype(F32) * HD_B ** -0.5
        s_w = jnp.where(valid, s_w, -jnp.inf)
        s_c = jnp.einsum('bqngd,bknd->bngqk', qb, k_ctx).astype(F32) * HD_B ** -0.5
        s = jnp.concatenate([s_w, s_c, jnp.broadcast_to(sink_l, s_w.shape[:-1] + (1,))], -1)
        pr = jax.nn.softmax(s, axis=-1).astype(v.dtype)
        return (jnp.einsum('bngqk,bknd->bqngd', pr[..., :span], vw)
                + jnp.einsum('bngqk,bknd->bqngd', pr[..., span:-1], v_ctx))
    return map_query_blocks(blk, qg).reshape(b, l, H_B * HD_B)

def odd_inputs(h, w_in, qn_w, kn_w):
    b, l = h.shape[:2]
    q, k, v = split_cols(h @ w_in, (ODD_W, ODD_W, ODD_W))
    q = rms_norm(q.reshape(b, l, H_C, 2, HD_C), qn_w)
    k = rms_norm(k.reshape(b, l, H_C, 2, HD_C), kn_w)
    return q, k, v.reshape(b, l, H_C, 2 * HD_C)

def rope_2d_pairs(x):
    b, l = x.shape[:2]
    return rope_2d(x.reshape(b, l, H_C * 2, HD_C)).reshape(x.shape)

def diff_lambda(lam_p, lam_init):
    lp = lam_p.astype(F32)
    return jnp.exp(jnp.sum(lp[0] * lp[1])) - jnp.exp(jnp.sum(lp[2] * lp[3])) + lam_init

def diff_attention(q, k_parts, v_parts, lam):
    sizes = [kp.shape[1] for kp in k_parts]
    def blk(qb, _i):
        s = jnp.concatenate([jnp.einsum('bqhcd,bkhcd->bhcqk', qb, kp) for kp in k_parts], -1)
        pr = jax.nn.softmax(s.astype(F32) * HD_C ** -0.5, axis=-1)
        w = (pr[:, :, 0] - lam * pr[:, :, 1]).astype(v_parts[0].dtype)
        terms, start = [], 0
        for vp, n in zip(v_parts, sizes):
            terms.append(jnp.einsum('bhqk,bkhe->bqhe', w[..., start:start + n], vp))
            start += n
        return sum(terms[1:], terms[0])
    return map_query_blocks(blk, q)

def diff_out(o, subln_w, lam_init, w_out):
    o = rms_norm(o, subln_w) * (1.0 - lam_init)
    return o.reshape(o.shape[0], o.shape[1], -1) @ w_out

def lambda_init_of(li):
    return 0.8 - 0.6 * math.exp(-0.3 * li)

def lower_bounds(lb_logits):
    sm = jax.nn.softmax(lb_logits.astype(F32), axis=0)
    return jnp.cumsum(sm, axis=0) - sm[0]

def even_layer_ctx(h, p, j, lbs):
    (q_r, g_f, g_b, v_r, gate), (q_a, k_a, v_a) = even_inputs(
        h, p['w_in_even'][j], lbs[j], p['swa_qnorm_w'][j], p['swa_knorm_w'][j])
    zeros = jnp.zeros((h.shape[0], H_A, DK_A, DV_A), F32)
    o_r, s_ctx = hgrn_bidir(q_r, g_f, g_b, v_r, zeros, zeros)
    out_a = hgrn_readout(o_r, gate, p['hgrn_norm_w'][j])
    out_b = swa_context_attention(q_a, k_a, v_a, p['swa_sink'][j])
    y = jnp.concatenate([out_a, out_b.astype(out_a.dtype)], -1) @ p['w_out_even'][j]
    return y, k_a, v_a, s_ctx.astype(h.dtype)

def even_layer_lat(h, p, j, lbs, k_ctx, v_ctx, s_ctx):
    (q_r, g_f, g_b, v_r, gate), (q_a, k_a, v_a) = even_inputs(
        h, p['w_in_even'][j], lbs[j], p['swa_qnorm_w'][j], p['swa_knorm_w'][j])
    s0 = s_ctx.astype(F32)
    o_r, _ = hgrn_bidir(q_r, g_f, g_b, v_r, s0[:, 0], s0[:, 1])
    out_a = hgrn_readout(o_r, gate, p['hgrn_norm_w'][j])
    out_b = swa_latent_attention(rope_2d(q_a), rope_2d(k_a), v_a, k_ctx, v_ctx, p['swa_sink'][j])
    return jnp.concatenate([out_a, out_b.astype(out_a.dtype)], -1) @ p['w_out_even'][j]

def odd_layer_ctx(h, p, j, li):
    q, k, v = odd_inputs(h, p['w_in_odd'][j], p['diff_qnorm_w'][j], p['diff_knorm_w'][j])
    lam_init = lambda_init_of(li)
    o = diff_attention(q, [k], [v], diff_lambda(p['diff_lambda_p'][j], lam_init))
    return diff_out(o, p['diff_subln_w'][j], lam_init, p['w_out_odd'][j]), k, v

def odd_layer_lat(h, p, j, li, k_ctx, v_ctx):
    q, k, v = odd_inputs(h, p['w_in_odd'][j], p['diff_qnorm_w'][j], p['diff_knorm_w'][j])
    lam_init = lambda_init_of(li)
    o = diff_attention(rope_2d_pairs(q), [rope_2d_pairs(k), k_ctx], [v, v_ctx],
                       diff_lambda(p['diff_lambda_p'][j], lam_init))
    return diff_out(o, p['diff_subln_w'][j], lam_init, p['w_out_odd'][j])

def sq_relu_mlp(h, w1, w2):
    return jnp.square(jax.nn.relu(h @ w1)) @ w2

def context_trunk(x, c_ctx, p):
    lbs = lower_bounds(p['hgrn_lb_logits'])
    cvec = c_ctx[None, :]
    ks, vs, ss, kd, vd = [], [], [], [], []
    for li in range(DEPTH):
        sh1, sc1, g1, sh2, sc2, g2 = ada_mods(cvec, p['w_ada'][li], p['b_ada'][li])
        h = rms_norm(x, p['norm_w'][li, 0]) * (1 + sc1) + sh1
        j = li // 2
        if li % 2 == 0:
            y, k, v, s = even_layer_ctx(h, p, j, lbs)
            ks.append(k); vs.append(v); ss.append(s)
        else:
            y, k, v = odd_layer_ctx(h, p, j, li)
            kd.append(k); vd.append(v)
        x = x + g1 * y
        h = rms_norm(x, p['norm_w'][li, 1]) * (1 + sc2) + sh2
        x = x + g2 * sq_relu_mlp(h, p['w_mlp1'][li], p['w_mlp2'][li])
    return (x, jnp.stack(ks, 1), jnp.stack(vs, 1), jnp.stack(ss, 1),
            jnp.stack(kd, 1), jnp.stack(vd, 1))

def latent_trunk(x, c, cache_k_swa, cache_v_swa, state_hgrn, cache_k_diff, cache_v_diff, p):
    lbs = lower_bounds(p['hgrn_lb_logits'])
    for li in range(DEPTH):
        sh1, sc1, g1, sh2, sc2, g2 = ada_mods(c, p['w_ada'][li], p['b_ada'][li])
        h = rms_norm(x, p['norm_w'][li, 0]) * (1 + sc1) + sh1
        j = li // 2
        if li % 2 == 0:
            y = even_layer_lat(h, p, j, lbs, cache_k_swa[:, j], cache_v_swa[:, j], state_hgrn[:, j])
        else:
            y = odd_layer_lat(h, p, j, li, cache_k_diff[:, j], cache_v_diff[:, j])
        x = x + g1 * y
        h = rms_norm(x, p['norm_w'][li, 1]) * (1 + sc2) + sh2
        x = x + g2 * sq_relu_mlp(h, p['w_mlp1'][li], p['w_mlp2'][li])
    return x

def setup_inputs(seed: int = 0) -> dict:
    key = jax.random.key(seed)
    ks = jax.random.split(key, 27)
    D = D_MODEL
    def nrm(k, shape, scale=1.0):
        return scale * jax.random.normal(k, shape, F32)
    return {
        'x_prompt': nrm(ks[0], (BATCH, SEQ, D)),
        'x_sample': nrm(ks[1], (DEC_BATCH, DEC_SEQ, D)),
        'cache_k_swa': nrm(ks[2], (DEC_BATCH, N_EVEN, PAST_LEN, KV_B, HD_B)),
        'cache_v_swa': nrm(ks[3], (DEC_BATCH, N_EVEN, PAST_LEN, KV_B, HD_B)),
        'state_hgrn': nrm(ks[4], (DEC_BATCH, N_EVEN, 2, H_A, DK_A, DV_A), 0.5),
        'cache_k_diff': nrm(ks[5], (DEC_BATCH, N_ODD, PAST_LEN, H_C, 2, HD_C)),
        'cache_v_diff': nrm(ks[6], (DEC_BATCH, N_ODD, PAST_LEN, H_C, 2 * HD_C)),
        'c': nrm(ks[7], (DEC_BATCH, D)),
        'c_ctx': nrm(ks[8], (D,)),
        'norm_w': 1.0 + nrm(ks[9], (DEPTH, 2, D), 0.02),
        'w_ada': nrm(ks[10], (DEPTH, D, 6 * D), 0.5 * D ** -0.5),
        'b_ada': nrm(ks[11], (DEPTH, 6 * D), 0.01),
        'w_in_even': nrm(ks[12], (N_EVEN, D, EVEN_COLS), D ** -0.5),
        'w_out_even': nrm(ks[13], (N_EVEN, D_MIX, D), D_MIX ** -0.5),
        'hgrn_lb_logits': nrm(ks[14], (N_EVEN, 2, F_A), 0.5),
        'hgrn_norm_w': 1.0 + nrm(ks[15], (N_EVEN, DV_A), 0.02),
        'swa_qnorm_w': 1.0 + nrm(ks[16], (N_EVEN, HD_B), 0.02),
        'swa_knorm_w': 1.0 + nrm(ks[17], (N_EVEN, HD_B), 0.02),
        'swa_sink': nrm(ks[18], (N_EVEN, H_B), 0.5),
        'w_in_odd': nrm(ks[19], (N_ODD, D, ODD_COLS), D ** -0.5),
        'w_out_odd': nrm(ks[20], (N_ODD, ODD_W, D), ODD_W ** -0.5),
        'diff_qnorm_w': 1.0 + nrm(ks[21], (N_ODD, HD_C), 0.02),
        'diff_knorm_w': 1.0 + nrm(ks[22], (N_ODD, HD_C), 0.02),
        'diff_lambda_p': nrm(ks[23], (N_ODD, 4, HD_C), 0.1),
        'diff_subln_w': 1.0 + nrm(ks[24], (N_ODD, 2 * HD_C), 0.02),
        'w_mlp1': nrm(ks[25], (DEPTH, D, D_FF), D ** -0.5),
        'w_mlp2': nrm(ks[26], (DEPTH, D_FF, D), D_FF ** -0.5),
    }

def reference(x_prompt, x_sample, cache_k_swa, cache_v_swa, state_hgrn, cache_k_diff, cache_v_diff,
              c, c_ctx, norm_w, w_ada, b_ada, w_in_even, w_out_even, hgrn_lb_logits, hgrn_norm_w,
              swa_qnorm_w, swa_knorm_w, swa_sink, w_in_odd, w_out_odd, diff_qnorm_w, diff_knorm_w,
              diff_lambda_p, diff_subln_w, w_mlp1, w_mlp2):
    p = dict(norm_w=norm_w, w_ada=w_ada, b_ada=b_ada, w_in_even=w_in_even, w_out_even=w_out_even,
             hgrn_lb_logits=hgrn_lb_logits, hgrn_norm_w=hgrn_norm_w, swa_qnorm_w=swa_qnorm_w,
             swa_knorm_w=swa_knorm_w, swa_sink=swa_sink, w_in_odd=w_in_odd, w_out_odd=w_out_odd,
             diff_qnorm_w=diff_qnorm_w, diff_knorm_w=diff_knorm_w, diff_lambda_p=diff_lambda_p,
             diff_subln_w=diff_subln_w, w_mlp1=w_mlp1, w_mlp2=w_mlp2)
    y_prompt, new_k_swa, new_v_swa, new_state_hgrn, new_k_diff, new_v_diff = context_trunk(x_prompt, c_ctx, p)
    y_sample = latent_trunk(x_sample, c, cache_k_swa, cache_v_swa, state_hgrn, cache_k_diff, cache_v_diff, p)
    return (y_prompt, y_sample, new_k_swa, new_v_swa, new_state_hgrn, new_k_diff, new_v_diff)


_drawn_inputs = setup_inputs


def setup_inputs(seed=0):
    import zlib

    import numpy as np

    out = dict(_drawn_inputs(seed))
    spreads = {}
    factors = {'cache_k_swa': 5.718,
     'cache_v_swa': 4.376,
     'state_hgrn': 8.0,
     'hgrn_norm_w': 8.0,
     'swa_qnorm_w': 8.0,
     'swa_knorm_w': 2.908,
     'swa_sink': 8.0,
     'diff_qnorm_w': 8.0,
     'diff_knorm_w': 3.52,
     'diff_subln_w': 32.994,
     'cache_k_diff': 8.0,
     'cache_v_diff': 8.0}
    for name, (base, spread) in spreads.items():
        noise = np.random.default_rng([zlib.crc32(name.encode()), seed]).standard_normal(out[name].shape)
        drawn = base * np.exp(spread * noise) if base else spread * noise
        out[name] = jnp.asarray(drawn.astype(out[name].dtype))
    for name, factor in factors.items():
        out[name] = (out[name] * factor).astype(out[name].dtype)
    return out
```

```python
import math
from contextlib import ExitStack

import numpy as np
import concourse.bass as bass
from concourse import mybir

F32 = mybir.dt.float32
F32R = mybir.dt.float32r
BF16 = mybir.dt.bfloat16
U8 = mybir.dt.uint8
I32 = mybir.dt.int32
ALU = mybir.AluOpType
ACT = mybir.ActivationFunctionType
AX = mybir.AxisListType

P = 128
D = 1024
KT = D // P
NTOK = 384
TT = NTOK // P
UC = 256
EPS = 1e-6
H_A, H_B, H_C, HD = 4, 8, 8, 64
GRID_W = 64
LAM_INIT = 0.8 - 0.6 * math.exp(-0.3 * 1)
RAW = 4
LEVELS = 7

Z_F, Z_B, Q_A, Q_SWA, KV_SWA, V_A, GATE = (0, 1), (2, 3), (4, 5), (6, 7), (8,), (9, 10), (11, 12)
EVEN_COLS = [512, 768, 1024, 1280, 0, 256, 2560, 2816, 3072, 1536, 1792, 2048, 2304]
ODD_COLS = [part * 1024 + UC * j for j in range(4) for part in range(3)]
U_EVEN, U_OUT_E, U_MLP0, U_ODD, U_OUT_O, U_MLP1 = 0, 13, 17, 49, 61, 65
N_UNITS = 97
ADA_COLS = 24
SH1, SC1, G1, SH2, SC2, G2 = range(6)

STREAM = [("a", a) for a in range(8)]
for _u in range(16):
    STREAM += [("u", _u), ("a", 8 + _u)]
STREAM += [("u", 16)]
for _i in range(24):
    STREAM += [("u", U_MLP0 + _i), ("a", 24 + _i)]
STREAM += [("u", _u) for _u in range(U_MLP0 + 24, N_UNITS)]
POS = {item: n for n, item in enumerate(STREAM)}

N_HG = 2 * (LEVELS + 1)
N_SWA = 12
EVEN_SIDE = {(6, 1): ["hg0"], (7, 1): ["hg1", "hg2"], (8, 1): ["tq", "hg3", "hg4"]}
_swa = 0
for _n in range(8):
    EVEN_SIDE[(9 + _n // 2, _n % 2)] = [f"hg{5 + _n}", f"swa{_swa}"]
    _swa += 1
EVEN_TAIL = ["hg13", f"swa{_swa}", "hg14", f"swa{_swa + 1}", "hg15", f"swa{_swa + 2}", "tile",
             f"swa{_swa + 3}", f"swa{_swa + 4}"]
EVEN_JOBS = [j for n in range(2 * 13) for j in EVEN_SIDE.get((n // 2, n % 2), [])] + EVEN_TAIL

N_DIFF = 3 * H_C


def job(name):
    kind = name.rstrip("0123456789")
    return kind, int(name[len(kind):] or 0)


def psum_uses():
    sc, tb, ob = [], ["vecs0", "vecs1"], []
    tb += [f"x{t}" for t in range(KT)]
    ob.append("norm0")
    ob += [f"ada{a}" for a in range(8)]
    tb += [f"ada{a}" for a in range(8)]

    def swa(s):
        if s >= 1:
            tb.extend([f"swaP{s - 1}.0", f"swaP{s - 1}.1"])
        if s < N_SWA:
            sc.append(f"swa{s}")
        if s >= 1:
            ob.append(f"swaO{s - 1}")

    def even_jobs(jobs):
        for name in jobs:
            kind, i = job(name)
            if kind == "hg":
                sc.append(name)
            elif kind == "tq":
                tb.extend([f"tq{j}" for j in range(4)] + ["tk"])
            elif kind == "tile":
                sc.append("att8")
                tb.extend(["kf_turned", "kb_turned"])
                ob.extend(["state_f", "state_b"])
            else:
                swa(i)

    for u in range(13):
        ob.append(f"ada{8 + u}")
        even_jobs(EVEN_SIDE.get((u, 0), []))
        even_jobs(EVEN_SIDE.get((u, 1), []))
        tb.append(f"ada{8 + u}")
    even_jobs(EVEN_TAIL)
    for h in range(H_A):
        ob.append(f"hgO{h}")
        tb.append(f"hgN{h}")
    for u in range(13, 16):
        ob.append(f"ada{8 + u}")
        tb.append(f"ada{8 + u}")
    ob.append("norm1")
    for a in range(24, 48):
        ob.append(f"ada{a}")
        tb.append(f"ada{a}")
    ob.append("norm2")

    def diff(s):
        if s >= 1:
            tb.append(f"dP{s - 1}")
        if s < N_DIFF:
            sc.append(f"d{s}")
        if s >= 1 and (s - 1) % 3 == 2:
            h = (s - 1) // 3
            ob.append(f"dO{h}")
            tb.append(f"dN{h}")

    for u in range(12):
        for half in range(2):
            for s in odd_slots(u, half):
                diff(s)
        tb.extend(odd_turns(u))
    for s in odd_slots(12, 0):
        diff(s)
    ob.append("norm3")
    tb.extend([f"y{n}" for n in range(6)])
    return [{name: n for n, name in enumerate(uses)} for uses in (sc, tb, ob)]


def odd_slots(u, half):
    if u == 12:
        return list(range(18, N_DIFF + 1))
    j = u // 3
    return [] if j == 0 else [6 * (j - 1) + 2 * (u % 3) + half]


def odd_turns(u):
    names = [f"t{u - 1}.0", f"t{u - 1}.1"] if u >= 1 and (u - 1) % 3 < 2 else []
    return names + (["kc0", "kc1"] if u == 2 else [])


SC_USE, TB_USE, OB_USE = psum_uses()


def step_backbone_kernel(nc, t):
    ctx = ExitStack()
    with ctx:
        def sb(name, shape, dt=F32):
            return ctx.enter_context(nc.sbuf_tensor(name, shape, dt))

        def sem(name):
            return ctx.enter_context(nc.semaphore(name))

        xT = sb("xT", [P, KT, NTOK])
        opH = sb("opH", [P, KT, NTOK], F32R)
        opL = sb("opL", [P, KT, NTOK], F32R)
        raw = sb("raw", [P, RAW, KT, UC])
        wH = sb("wH", [P, 2, KT, UC], F32R)
        wL = sb("wL", [P, 2, KT, UC], F32R)
        nbuf = sb("nbuf", [P, 2, NTOK])
        rstd = sb("rstd", [P, NTOK])
        ident = sb("ident", [P, P])
        ones = sb("ones", [P, P])
        vecs = sb("vecs", [P, P + 32])
        cst = sb("cst", [P, KT, 32])
        mods = sb("mods", [P, 2, 48, 2])
        scale1 = sb("scale1", [P, 4, KT, 2])
        adarow = sb("adarow", [P, UC])
        small = sb("small", [P, 128])
        epsc = sb("epsc", [P, 1])
        trig = sb("trig", [P, 2, 2, HD])
        wrow = sb("wrow", [P, 4, HD])

        def arena(parts):
            held = [nc.sbuf_tensor(name, shape, dt) for name, shape, dt in parts]
            got = [h.__enter__() for h in held]
            for h in reversed(held):
                h.__exit__(None, None, None)
            return got

        xin, vrow0, vrow1 = arena([("xin", [P, TT, D], F32), ("vrow0", [P, P], F32), ("vrow1", [32, P], F32)])
        (X, hq, kk, E, vtok, att, qout, kout, vout, qT, kT, PB, PT, obuf, S0, swaK, swaV, ropeE, masks,
         wmask, idbf) = arena([
            ("X", [P, 2, 12, 129], F32),
            ("hq", [P, 12, P], F32),
            ("kk", [P, 2, 12, P], F32),
            ("E", [P, 2, 2048], F32),
            ("vtok", [P, TT, 512], F32),
            ("att", [P, 12, P], F32),
            ("qout", [P, TT, 512], F32),
            ("kout", [P, TT, P], F32),
            ("vout", [P, TT, P], F32),
            ("qT", [P, 4, NTOK], F32),
            ("kT", [P, 512], F32),
            ("PB", [P, 768], F32),
            ("PT", [P, 768], F32),
            ("obuf", [P, 4, NTOK], F32),
            ("S0", [P, 2, 4, P], F32),
            ("swaK", [P, P], F32),
            ("swaV", [P, P], F32),
            ("ropeE", [P, 2, 2, 2, HD], F32),
            ("masks", [P, 8, P], U8),
            ("wmask", [P, 2, P], BF16),
            ("idbf", [P, P], BF16)])
        hidH, hidL, relu, relu2 = arena([("hidH", [P, KT, NTOK], F32R), ("hidL", [P, KT, NTOK], F32R),
                                         ("relu", [P, 2, 2 * NTOK], F32), ("relu2", [P, 2, 2 * NTOK], F32)])
        (dqT, dkT, dv, dkc, dvc, draw, dsq, dout, DP, DW, DPT, doT, ropeO, lamp) = arena([
            ("dqT", [P, H_C, NTOK], F32),
            ("dkT", [P, H_C, 512], F32),
            ("dv", [P, TT, D], F32),
            ("dkc", [P, D], F32),
            ("dvc", [P, D], F32),
            ("draw", [P, 768], F32),
            ("dsq", [P, 768], F32),
            ("dout", [P, 2, TT, UC], F32),
            ("DP", [P, 2, NTOK], F32),
            ("DW", [P, NTOK], F32),
            ("DPT", [P, NTOK], F32),
            ("doT", [P, H_C, NTOK], F32),
            ("ropeO", [P, 2, 2, 2, HD], F32),
            ("lamp", [P, 4, HD], F32)])
        (yout,) = arena([("yout", [P, TT, D], F32)])
        sb("arena_end", [P, 1])

        G = ctx.enter_context(nc.psum_tensor("G", [P, 2, 1024], F32))
        SC = ctx.enter_context(nc.psum_tensor("SC", [P, 1024], F32))
        TB = ctx.enter_context(nc.psum_tensor("TB", [P, 512], F32))
        OB = ctx.enter_context(nc.psum_tensor("OB", [P, 512], F32))

        normw = vecs[:, 0:32].rearrange("p (n t) -> p n t", n=4)
        bada = vecs[:, 32:128].rearrange("p (l i) -> p l i", l=2)
        c2 = vecs[:, P:P + 16].rearrange("p (c t) -> p c t", c=2)
        lbl = vecs[:, P + 16:P + 24]
        hgw = vecs[:, P + 24:P + 25]
        subw = vecs[:, P + 25:P + 26]
        lb, omlb = small[:, 0:8], small[:, 8:16]
        sgt = small[:, 16:32]
        ss, rs = small[:, 32:44], small[:, 44:56]
        sinkb = small[:, 56:64]
        mx, negm, dsink = small[:, 64:66], small[:, 66:68], small[:, 68:70]
        ssum, esink, den, rden = small[:, 70:72], small[:, 72:74], small[:, 74:76], small[:, 76:78]
        tot = small[:, 78:86].rearrange("p (d h) -> p d h", d=2)
        lam2, lam = small[:, 86:88], small[:, 88:89]
        subs = small[:, 90:91]
        gcp = small[:, 92:96]
        adat = small[:, 96:100].rearrange("p (i c) -> p i c", c=2)

        const_in, x_in, vec_in, even_in, odd_in, out_dma, kd_out = (
            sem(n) for n in ("const_in", "x_in", "vec_in", "even_in", "odd_in", "out_dma", "kd_out"))
        raw_in = [sem(f"raw_in{i}") for i in range(RAW)]
        w_high, w_split, gemm_done = sem("w_high"), sem("w_split"), sem("gemm_done")
        g_free = [sem(f"g_free{i}") for i in range(2)]
        sc_full, sc_free = sem("sc_full"), sem("sc_free")
        tb_full, tb_free = sem("tb_full"), sem("tb_free")
        ob_full, ob_free = sem("ob_full"), sem("ob_free")
        dve_step, act_step, pool_step = sem("dve_step"), sem("act_step"), sem("pool_step")
        ones_set, cst_zero, cexp_set, lbmax_sub, cst_set, mods_set = (
            sem(n) for n in ("ones_set", "cst_zero", "cexp_set", "lbmax_sub", "cst_set", "mods_set"))
        sq_set, sq_used, rstd_set = sem("sq_set"), sem("sq_used"), sem("rstd_set")
        scaled_set, oph_set, op_set = sem("scaled_set"), sem("oph_set"), sem("op_set")
        sig_set, f_set, logf_set, k_set, scans_done, silu_sig = (
            sem(n) for n in ("sig_set", "f_set", "logf_set", "k_set", "scans_done", "silu_sig"))
        hg_arg, hg_exp, hg_mul = sem("hg_arg"), sem("hg_exp"), sem("hg_mul")
        tile_arg, tile_exp, tile_mul, s0_set = (sem(n) for n in ("tile_arg", "tile_exp", "tile_mul", "s0_set"))
        rope_tab, ss_set, rs_set, xr_set, rope_set = (
            sem(n) for n in ("rope_tab", "ss_set", "rs_set", "xr_set", "rope_set"))
        negm_set, exp_set, p_set = sem("negm_set"), sem("exp_set"), sem("p_set")
        dnegm_set, dw_set, lamr_set, lam_exp = sem("dnegm_set"), sem("dw_set"), sem("lamr_set"), sem("lam_exp")
        ro_rstd, ro_set = sem("ro_rstd"), sem("ro_set")
        relu_sq, relu2_set, hid_set = sem("relu_sq"), sem("relu2_set"), sem("hid_set")

        block = ctx.enter_context(nc.Block())

        def unit_cols(w, col):
            return w[:, col:col + UC].rearrange("(k p) n -> p k n", p=P)

        @block.sync
        def _(sp):
            def load(src, pos, wait=None):
                if wait is not None:
                    sp.wait_ge(*wait)
                elif pos >= RAW:
                    kind, n = STREAM[pos - RAW]
                    if kind == "u":
                        sp.wait_ge(w_split, n + 1)
                    else:
                        sp.wait_ge(ob_free, OB_USE[f"ada{n}"] + 1)
                sp.dma_start(raw[:, pos % RAW, :, :], src).then_inc(raw_in[pos % RAW], 16)

            def load_ada(a):
                load(unit_cols(t["w_ada"][a // ADA_COLS], (a % ADA_COLS) * UC), POS["a", a])

            def mlp_unit(layer, i, g):
                if i < 4:
                    src = t["w_mlp1"][layer][:, bass.ds(g * D + i * UC, UC)]
                else:
                    src = t["w_mlp2"][layer][bass.ds(g * D, D), (i - 4) * UC:(i - 3) * UC]
                return src.rearrange("(k p) n -> p k n", p=P)

            for a in range(4):
                load_ada(a)
            sp.dma_start(xin[:, 1:3, :], t["x_sample"][0].rearrange("(a p) d -> p a d", p=P)).then_inc(x_in, 16)
            for a in range(4, 8):
                load_ada(a)
            for u in range(13):
                load(unit_cols(t["w_in_even"][0], EVEN_COLS[u]), POS["u", u])
                load_ada(8 + u)
            for u in range(13, 17):
                load(unit_cols(t["w_out_even"][0], (u - 13) * UC), POS["u", u])
                if u < 16:
                    load_ada(8 + u)
            sp.wait_ge(ob_free, OB_USE["ada23"] + 1)
            with sp.Fori(0, 3) as g:
                for i in range(8):
                    load(mlp_unit(0, i, g), POS["u", U_MLP0] + 2 * i, (w_split, U_MLP0 + i - 1 + 8 * g))
                    src = t["w_ada"][1][:, bass.ds(g * (8 * UC) + i * UC, UC)].rearrange("(k p) n -> p k n", p=P)
                    load(src, POS["a", 24] + 2 * i, (ob_free, OB_USE["ada24"] + i - 1 + 8 * g))
            for i in range(8):
                load(mlp_unit(0, i, 3), POS["u", U_MLP0 + 24 + i])
            for u in range(12):
                load(unit_cols(t["w_in_odd"][0], ODD_COLS[u]), POS["u", U_ODD + u])
            for u in range(4):
                load(unit_cols(t["w_out_odd"][0], u * UC), POS["u", U_OUT_O + u])
            with sp.Fori(0, 4) as g:
                for i in range(8):
                    load(mlp_unit(1, i, g), POS["u", U_MLP1] + i, (w_split, U_MLP1 + i - 3 + 8 * g))
            sp.wait_ge(tb_free, TB_USE["y5"] + 1)
            sp.dma_start(t["y_prompt"][0], yout[:, 0, :]).then_inc(out_dma, 16)
            sp.dma_start(t["y_sample"][0].rearrange("(a p) d -> p a d", p=P), yout[:, 1:3, :]).then_inc(out_dma, 16)
            sp.wait_ge(out_dma, 16 * 6)
            sp.wait_ge(kd_out, 16 * 4)

        @block.tensor
        def _(pe):
            def take(buf, name):
                uses, free = {"sc": (SC_USE, sc_free), "tb": (TB_USE, tb_free), "ob": (OB_USE, ob_free)}[buf]
                if uses[name]:
                    pe.wait_ge(free, uses[name])

            def turn(out, src, n=P):
                return pe.transpose(out, src, ident[0:n, 0:n])

            def gemm_half(u, half, form, moving, ready=None, order=range(KT), g=0):
                mH, mL = moving
                s = u % 2
                if half == 0:
                    pe.wait_ge(w_split, u + 1 + 8 * g)
                    if u >= 2:
                        pe.wait_ge(g_free[s], u // 2 + 4 * g)
                mm = None
                for n in range(4 * half, 4 * half + 4):
                    k = order[n]
                    if ready is not None:
                        ready(n)
                    first, last = n == 0, n == KT - 1
                    passes = ((wH, mH), (wH, mL), (wL, mH))
                    if form == "fm":
                        for m in range(2):
                            for q, (w, a) in enumerate(passes):
                                mm = pe.matmul(G[:, s, 512 * m:512 * m + NTOK], w[:, s, k, P * m:P * m + P],
                                               a[:, k, :], start=first and q == 0, stop=last and q == 2)
                    else:
                        for tt in range(TT):
                            for q, (w, a) in enumerate(passes):
                                mm = pe.matmul(G[:, s, UC * tt:UC * tt + UC], a[:, k, P * tt:P * tt + P],
                                               w[:, s, k, :], start=first and q == 0 and tt != 1,
                                               stop=last and q == 2, skip_group_check=True)
                if half == 1:
                    mm.then_inc(gemm_done, 1)

            def ada_mm(slot, pos_wait, n_ob):
                pe.wait_ge(raw_in[slot], pos_wait)
                pe.wait_ge(ob_free, n_ob)
                for k in range(KT):
                    j = k % 4
                    mm = pe.matmul(OB[32 * j:32 * j + 32, 0:UC], cst[:, k, :], raw[:, slot, k, :],
                                   start=k < 4, stop=k >= 4, skip_group_check=True, tile_position=(0, 32 * j))
                mm.then_inc(ob_full, 1)

            def ada_turn(n_ob, n_tb):
                pe.wait_ge(ob_free, n_ob + 1)
                pe.wait_ge(tb_free, n_tb)
                for i in range(2):
                    mm = turn(TB[:, P * i:P * i + P], adarow[:, P * i:P * i + P])
                mm.then_inc(tb_full, 1)

            def ada(a, what):
                pos = POS["a", a]
                if what == "mm":
                    ada_mm(pos % RAW, 16 * (pos // RAW + 1), OB_USE[f"ada{a}"])
                else:
                    ada_turn(OB_USE[f"ada{a}"], TB_USE[f"ada{a}"])

            def norm_sum(n):
                take("ob", f"norm{n}")
                for k in range(KT):
                    pe.wait_ge(sq_set, KT * n + k + 1)
                    mm = pe.matmul(OB[:, 0:NTOK], ones[:, :], nbuf[:, k % 2, :], start=k == 0, stop=k == KT - 1)
                    mm.then_inc(ob_full if k == KT - 1 else sq_used, 1)

            pe.wait_ge(vec_in, 16 * 8)
            pe.wait_ge(const_in, 16)
            turn(TB[:, 0:P], vrow0[:, :]).then_inc(tb_full, 1)
            take("tb", "vecs1")
            turn(TB[:, 0:32], vrow1[:, :], 32).then_inc(tb_full, 1)
            pe.wait_ge(x_in, 32)
            for k in range(KT):
                take("tb", f"x{k}")
                for tt in range(TT):
                    mm = turn(TB[:, P * tt:P * tt + P], xin[:, tt, P * k:P * k + P])
                mm.then_inc(tb_full, 1)
            pe.wait_ge(ones_set, 1)
            norm_sum(0)
            pe.wait_ge(cst_set, 1)
            for a in range(8):
                ada(a, "mm")
                ada(a, "turn")

            def op_ready(n_before):
                return lambda n: pe.wait_ge(op_set, n_before + n + 1)

            def hg(i):
                grp, lev = i % 2, i // 2
                take("sc", f"hg{i}")
                pe.wait_ge(hg_mul, i + 1)
                for m in range(6):
                    q = hq[:, 6 * grp + m, :] if lev == LEVELS else E[:, grp, P * m:P * m + P]
                    mm = pe.matmul(SC[:, P * m:P * m + P], E[:, grp, 1024 + P * m:1024 + P * m + P], q,
                                   start=True, stop=True, skip_group_check=True)
                mm.then_inc(sc_full, 1)

            def keys_of(ti):
                return (0, P) if ti == 0 else (P, 512)

            def swa(s):
                if s >= 1:
                    b = s - 1
                    ti = b // 4
                    lo, hi = keys_of(ti)
                    nt = (hi - lo) // P
                    for hh in range(2):
                        take("tb", f"swaP{b}.{hh}")
                        pe.wait_ge(p_set, b + 1)
                        for kt in range(nt):
                            mm = turn(TB[:, P * kt:P * kt + P], PB[:, NTOK * hh + P * kt:NTOK * hh + P * kt + P])
                        mm.then_inc(tb_full, 1)
                if s < N_SWA:
                    ti, pair = s // 4, s % 4
                    lo, hi = keys_of(ti)
                    take("sc", f"swa{s}")
                    pe.wait_ge(tb_free, TB_USE["tk"] + 1)
                    for hh in range(2):
                        h = 2 * pair + hh
                        b0 = 64 * (h // 4)
                        mm = pe.matmul(SC[:, 512 * hh:512 * hh + hi - lo], qT[b0:b0 + 64, h % 4, P * ti:P * ti + P],
                                       kT[b0:b0 + 64, lo:hi], start=True, stop=ti == 0, skip_group_check=True)
                        if ti:
                            off = 512 * hh + (P if ti == 1 else 0)
                            mm = pe.matmul(SC[:, off:off + P], idbf[:, :], wmask[:, ti - 1, :], start=False,
                                           stop=True, skip_group_check=True)
                    mm.then_inc(sc_full, 1)
                if s >= 1:
                    b = s - 1
                    ti, pair = b // 4, b % 4
                    lo, hi = keys_of(ti)
                    take("ob", f"swaO{b}")
                    kv = HD * (2 * pair // 4)
                    vals = [vout[:, 0, kv:kv + HD]] if ti == 0 else \
                        [vout[:, 1, kv:kv + HD], vout[:, 2, kv:kv + HD], swaV[:, kv:kv + HD]]
                    for hh in range(2):
                        pe.wait_ge(tb_free, TB_USE[f"swaP{b}.{hh}"] + 1)
                        for n, v in enumerate(vals):
                            mm = pe.matmul(OB[64 * hh:64 * hh + 64, 0:P], v, PT[:, NTOK * hh + P * n:NTOK * hh + P * n + P],
                                           start=n == 0, stop=n == len(vals) - 1, skip_group_check=True)
                    mm.then_inc(ob_full, 1)

            def turn_qk():
                pe.wait_ge(rope_set, 3)
                for j in range(4):
                    take("tb", f"tq{j}")
                    for tt in range(TT):
                        mm = turn(TB[:, P * tt:P * tt + P], qout[:, tt, P * j:P * j + P])
                    mm.then_inc(tb_full, 1)
                take("tb", "tk")
                pe.wait_ge(even_in, 16 * 6)
                for tt in range(TT):
                    turn(TB[:, P * tt:P * tt + P], kout[:, tt, :])
                turn(TB[:, NTOK:512], swaK[:, :]).then_inc(tb_full, 1)

            Eq, Ek = E[:, 0, :], E[:, 1, :]

            def hseg(e, part, h, n):
                return e[:, 1024 * part + UC * h + P * n:1024 * part + UC * h + P * n + P]

            def tile():
                take("sc", "att8")
                pe.wait_ge(tile_mul, 1)
                for h in range(H_A):
                    pe.matmul(SC[:, UC * h:UC * h + P], hseg(Ek, 1, h, 1), hseg(Eq, 1, h, 0),
                              start=True, stop=True, skip_group_check=True)
                    mm = pe.matmul(SC[:, UC * h + P:UC * h + UC], hseg(Ek, 0, h, 1), hseg(Eq, 0, h, 1),
                                   start=True, stop=True, skip_group_check=True)
                mm.then_inc(sc_full, 1)
                for d, name in enumerate(("kf_turned", "kb_turned")):
                    take("tb", name)
                    for h in range(H_A):
                        mm = turn(TB[:, P * h:P * h + P], hseg(Ek, d, h, 0))
                    mm.then_inc(tb_full, 1)
                for d, name in enumerate(("state_f", "state_b")):
                    take("ob", name)
                    pe.wait_ge(tb_free, TB_USE[("kf_turned", "kb_turned")[d]] + 1)
                    for h in range(H_A):
                        mm = pe.matmul(OB[:, P * h:P * h + P], kk[:, 1, 4 * d + h, :], vtok[:, 0, P * h:P * h + P],
                                       start=True, stop=True, skip_group_check=True)
                    mm.then_inc(ob_full, 1)

            def even_jobs(jobs):
                for name in jobs:
                    kind, i = job(name)
                    if kind == "hg":
                        hg(i)
                    elif kind == "swa":
                        swa(i)
                    elif kind == "tq":
                        turn_qk()
                    else:
                        tile()

            for u in range(13):
                ada(8 + u, "mm")
                form = "tok" if u in Q_SWA + KV_SWA + V_A else "fm"
                for half in range(2):
                    gemm_half(u, half, form, (opH, opL), op_ready(0) if u == 0 else None)
                    even_jobs(EVEN_SIDE.get((u, half), []))
                ada(8 + u, "turn")
            even_jobs(EVEN_TAIL)

            pe.wait_ge(sc_free, SC_USE["att8"] + 1)
            pe.wait_ge(s0_set, 1)

            def v_of(tt, h):
                return vtok[:, tt, P * h:P * h + P]

            def hg_norm(h):
                take("tb", f"hgN{h}")
                pe.wait_ge(ob_free, OB_USE[f"hgO{h}"] + 1)
                pe.matmul(TB[:, 0:NTOK], ones[:, :], nbuf[:, h % 2, :], start=True, stop=True).then_inc(tb_full, 1)

            S0s = X[:, 0, 0:8, 0:P]

            for h in range(H_A):
                take("ob", f"hgO{h}")
                sums = [[(v_of(0, h), att[:, 3 * h, :])],
                        [(v_of(1, h), att[:, 3 * h + 1, :]), (v_of(2, h), kk[:, 0, 2 * h, :]),
                         (S0[:, 0, h, :], hseg(Eq, 0, h, 0)), (S0s[:, 4 + h, :], hseg(Eq, 1, h, 0))],
                        [(v_of(2, h), att[:, 3 * h + 2, :]), (v_of(1, h), kk[:, 0, 2 * h + 1, :]),
                         (S0s[:, h, :], hseg(Eq, 0, h, 1)), (S0[:, 1, h, :], hseg(Eq, 1, h, 1))]]
                for tt, terms in enumerate(sums):
                    for n, (w, a) in enumerate(terms):
                        mm = pe.matmul(OB[:, P * tt:P * tt + P], w, a, start=n == 0, stop=n == len(terms) - 1,
                                       skip_group_check=True)
                mm.then_inc(ob_full, 1)
                if h:
                    hg_norm(h - 1)
            hg_norm(H_A - 1)

            SWA_FIRST = [4, 5, 6, 7, 0, 1, 2, 3]
            for u in range(13, 17):
                if u < 16:
                    ada(8 + u, "mm")
                for half in range(2):
                    gemm_half(u, half, "fm", (opH, opL), op_ready(KT) if u == 13 else None, SWA_FIRST)
                if u < 16:
                    ada(8 + u, "turn")
            norm_sum(1)

            def mlp_group(base, g, with_ada, n_op):
                for i in range(8):
                    if with_ada:
                        pos = POS["a", 24] + 2 * i
                        ada_mm(pos % RAW, 16 * (pos // RAW + 1) + 16 * (16 // RAW) * g,
                               OB_USE["ada24"] + i + 8 * g)
                    ready = None
                    if i == 0:
                        ready = op_ready(n_op)
                    if i == 4:
                        done = 16 if base == U_MLP1 else 0
                        ready = lambda n: pe.wait_ge(hid_set, done + 4 * g + n // 2 + 1) if n % 2 == 0 else None
                    for half in range(2):
                        gemm_half(base + i, half, "fm", (opH, opL) if i < 4 else (hidH, hidL), ready, g=g)
                    if with_ada:
                        ada_turn(OB_USE["ada24"] + i + 8 * g, TB_USE["ada24"] + i + 8 * g)

            with pe.Fori(0, 3) as g:
                mlp_group(U_MLP0, g, True, 2 * KT)
            mlp_group(U_MLP0, 3, False, 2 * KT)
            norm_sum(2)

            def diff(s):
                if s >= 1:
                    b = s - 1
                    lo, hi = keys_of(b % 3)
                    take("tb", f"dP{b}")
                    pe.wait_ge(dw_set, b + 1)
                    for kt in range((hi - lo) // P):
                        mm = turn(TB[:, P * kt:P * kt + P], DW[:, P * kt:P * kt + P])
                    mm.then_inc(tb_full, 1)
                if s < N_DIFF:
                    h, ti = s // 3, s % 3
                    lo, hi = keys_of(ti)
                    take("sc", f"d{s}")
                    pe.wait_ge(tb_free, TB_USE[f"t{3 * (h // 2) + 1}.1"] + 1)
                    for c in range(2):
                        mm = pe.matmul(SC[:, 512 * c:512 * c + hi - lo], dqT[64 * c:64 * c + 64, h, P * ti:P * ti + P],
                                       dkT[64 * c:64 * c + 64, h, lo:hi], start=True, stop=True)
                    mm.then_inc(sc_full, 1)
                if s >= 1:
                    b = s - 1
                    h, ti = b // 3, b % 3
                    if ti == 0:
                        take("ob", f"dO{h}")
                        pe.wait_ge(g_free[(U_ODD + 3 * (h // 2) + 2) % 2], (U_ODD + 3 * (h // 2) + 2) // 2 + 1)
                    pe.wait_ge(tb_free, TB_USE[f"dP{b}"] + 1)
                    vals = [dv[:, 0, P * h:P * h + P]] if ti == 0 else \
                        [dv[:, 1, P * h:P * h + P], dv[:, 2, P * h:P * h + P], dvc[:, P * h:P * h + P]]
                    for n, v in enumerate(vals):
                        mm = pe.matmul(OB[:, P * ti:P * ti + P], v, DPT[:, P * n:P * n + P], start=n == 0,
                                       stop=n == len(vals) - 1, skip_group_check=True)
                    if ti == 2:
                        mm.then_inc(ob_full, 1)
                        take("tb", f"dN{h}")
                        pe.wait_ge(ob_free, OB_USE[f"dO{h}"] + 1)
                        pe.matmul(TB[:, 0:NTOK], ones[:, :], nbuf[:, h % 2, :], start=True,
                                  stop=True).then_inc(tb_full, 1)

            def turns(u):
                for name in odd_turns(u):
                    take("tb", name)
                    if name.startswith("kc"):
                        pe.wait_ge(odd_in, 16 * 3)
                        for h in range(4):
                            c = D // 2 * int(name[2]) + P * h
                            mm = turn(TB[:, P * h:P * h + P], dkc[:, c:c + P])
                    else:
                        n = int(name[-1])
                        pe.wait_ge(rope_set, 3 + 2 * ((u - 1) // 3) + (u - 1) % 3 + 1)
                        for tt in range(TT):
                            mm = turn(TB[:, P * tt:P * tt + P], dout[:, (u - 1) % 3, tt, P * n:P * n + P])
                    mm.then_inc(tb_full, 1)

            for u in range(12):
                for half in range(2):
                    gemm_half(U_ODD + u, half, "tok", (opH, opL), op_ready(3 * KT) if u == 0 else None)
                    for s in odd_slots(u, half):
                        diff(s)
                turns(u)
            for s in odd_slots(12, 0):
                diff(s)
            for u in range(4):
                for half in range(2):
                    gemm_half(U_OUT_O + u, half, "fm", (opH, opL), op_ready(4 * KT) if u == 0 else None)
            norm_sum(3)
            with pe.Fori(0, 4) as g:
                mlp_group(U_MLP1, g, False, 5 * KT)
            for n in range(6):
                take("tb", f"y{n}")
                for u in (N_UNITS - 2, N_UNITS - 1):
                    pe.wait_ge(g_free[u % 2], u // 2 + 1)
                for q in range(4):
                    k = 4 * (n % 2) + q
                    mm = turn(TB[:, P * q:P * q + P], xT[:, k, P * (n // 2):P * (n // 2) + P])
                mm.then_inc(tb_full, 1)

        @block.scalar
        def _(act):
            steps = [0]

            def settle(ins):
                steps[0] += 1
                ins.then_inc(act_step, 1)
                act.wait_ge(act_step, steps[0])

            def full(buf, name):
                uses, filled = {"sc": (SC_USE, sc_full), "tb": (TB_USE, tb_full), "ob": (OB_USE, ob_full)}[buf]
                act.wait_ge(filled, uses[name] + 1)

            def unit_out(u, n_cols):
                act.wait_ge(gemm_done, u + 1)
                g = G[:, u % 2, :]
                return g.rearrange("p (m n) -> p m n", m=2)[:, :, 0:NTOK] if n_cols == "fm" else g[:, 0:3 * UC]

            def split_high(u, pos, g=0, per=0):
                act.wait_ge(raw_in[pos % RAW], 16 * (pos // RAW + 1) + 16 * (per // RAW) * g)
                if u >= 2:
                    act.wait_ge(gemm_done, u - 1 + 8 * g)
                act.activation(wH[:, u % 2, :, :], raw[:, pos % RAW, :, :], ACT.Copy).then_inc(w_high, 1)

            def split(u):
                if u < N_UNITS:
                    split_high(u, POS["u", u])

            def ada_copy(n_ob, g=0):
                act.wait_ge(ob_full, n_ob + 1 + 8 * g)
                act.activation(adarow[:, :], OB[:, 0:UC], ACT.Copy).then_inc(ob_free, 1)

            def norm(n, source_ready):
                for k in range(KT):
                    source_ready(k)
                    if k >= 2:
                        act.wait_ge(sq_used, (KT - 1) * n + k - 1)
                    act.activation(nbuf[:, k % 2, :], xT[:, k, :], ACT.Square).then_inc(sq_set, 1)
                full("ob", f"norm{n}")
                act.activation(rstd[:, :], OB[:, 0:NTOK], ACT.Ln, bias=epsc[:, :], scale=1.0 / D).then_inc(ob_free, 1)
                act.wait_ge(ob_free, OB_USE[f"norm{n}"] + 1)
                act.activation(rstd[:, :], rstd[:, :], ACT.Exp, scale=-0.5).then_inc(rstd_set, 1)

            def shift(n, n_op):
                part = SH1 if n % 2 == 0 else SH2
                for k in range(KT):
                    act.wait_ge(scaled_set, KT * n + k + 1)
                    for c, (a, b) in enumerate(((0, P), (P, NTOK))):
                        ins = act.activation(opH[:, k, a:b], nbuf[:, k % 2, a:b], ACT.Identity,
                                             bias=mods[:, n // 2, KT * part + k, c:c + 1])
                    ins.then_inc(oph_set, 1)

            act.dma_start(ident[:, :], t["ident"]).then_inc(const_in, 16)
            for part, src in ((vrow0[0:32, :], t["norm_w"].rearrange("l n (t q) -> (l n t) q", q=P)),
                              (vrow0[32:P, :], t["b_ada"].rearrange("l (i q) -> (l i) q", q=P)),
                              (vrow1[0:8, :], t["c_ctx"].rearrange("(i q) -> i q", q=P)),
                              (vrow1[8:16, :], t["c"].rearrange("o (i q) -> (o i) q", q=P)),
                              (vrow1[16:24, :], t["hgrn_lb_logits"].rearrange("o d (h q) -> (o d h) q", q=P)),
                              (vrow1[24:25, :], t["hgrn_norm_w"]),
                              (vrow1[25:26, :], t["diff_subln_w"]),
                              (vrow1[26:32, :], t["c_ctx"].rearrange("(i q) -> i q", q=P)[0:6, :])):
                act.dma_start(part, src).then_inc(vec_in, 16)
            act.dma_start(xin[:, 0, :], t["x_prompt"][0]).then_inc(x_in, 16)
            act.dma_start(wrow[:, 0, :], t["swa_qnorm_w"].broadcast_to([P, HD])).then_inc(even_in, 16)
            act.dma_start(wrow[:, 1, :], t["swa_knorm_w"].broadcast_to([P, HD])).then_inc(even_in, 16)
            act.dma_start(wrow[:, 2, :], t["diff_qnorm_w"].broadcast_to([P, HD])).then_inc(even_in, 16)
            act.dma_start(wrow[:, 3, :], t["diff_knorm_w"].broadcast_to([P, HD])).then_inc(even_in, 16)
            act.dma_start(sinkb, t["swa_sink"].broadcast_to([P, H_B])).then_inc(even_in, 16)
            act.dma_start(trig[:, :, :, :], t["trig"]).then_inc(even_in, 16)
            act.dma_start(masks[:, :, :].rearrange("p l k -> p (l k)").bitcast(I32), t["masks"]).then_inc(even_in, 16)
            act.dma_start(wmask[:, :, :].rearrange("p a k -> p (a k)").bitcast(I32), t["wmask"]).then_inc(even_in, 16)
            act.dma_start(idbf[:, :].bitcast(I32), t["idbf"]).then_inc(even_in, 16)
            act.dma_start(swaK[:, :], t["cache_k_swa"][0, 0].rearrange("s n d -> s (n d)")).then_inc(even_in, 16)
            act.dma_start(swaV[:, :], t["cache_v_swa"][0, 0].rearrange("s n d -> s (n d)")).then_inc(even_in, 16)
            act.dma_start(S0[:, :, :, :], t["state_hgrn"][0, 0].rearrange("d h k v -> k d h v")).then_inc(even_in, 16)
            full("tb", "vecs0")
            act.activation(vecs[:, 0:P], TB[:, 0:P], ACT.Copy).then_inc(tb_free, 1)
            full("tb", "vecs1")
            act.activation(vecs[:, P:P + 32], TB[:, 0:32], ACT.Copy).then_inc(tb_free, 1)
            act.wait_ge(tb_free, 2)
            act.activation(sgt, vecs[:, P:P + 16], ACT.Exp, scale=-1.0).then_inc(cexp_set, 1)
            act.wait_ge(lbmax_sub, 1)
            act.activation(lb, lb, ACT.Exp).then_inc(cexp_set, 1)
            for k in range(KT):
                full("tb", f"x{k}")
                act.activation(xT[:, k, :], TB[:, 0:NTOK], ACT.Copy).then_inc(tb_free, 1)
            act.wait_ge(ones_set, 1)
            norm(0, lambda k: act.wait_ge(tb_free, TB_USE[f"x{k}"] + 1))
            for a in range(8):
                ada_copy(OB_USE[f"ada{a}"])
            split(0)
            split(1)
            shift(0, 0)

            def gates(u):
                d, i = u // 2, u % 2
                if u >= 2:
                    act.wait_ge(scans_done, u - 1)
                    act.wait_ge(k_set, u - 1)
                e = kk[:, d, 6 * i:6 * i + 6, :].rearrange("p a b -> p (a b)")
                act.activation(e.rearrange("p (m n) -> p m n", m=2), unit_out(u, "fm"), ACT.Exp,
                               scale=-1.0).then_inc(g_free[u % 2], 1)
                act.wait_ge(g_free[u % 2], u // 2 + 1)
                settle(act.activation(e, e, ACT.Ln, bias=ones[:, 0:1]))
                act.activation(E[:, i, 0:768], e, ACT.Exp, scale=-1.0).then_inc(sig_set, 1)

            def log_gates(u):
                act.wait_ge(f_set, u + 1)
                act.activation(E[:, u % 2, 1024:1792], E[:, u % 2, 0:768], ACT.Ln).then_inc(logf_set, 1)

            def silu_part(dst, u):
                settle(act.activation(dst.rearrange("p (m n) -> p m n", m=2), unit_out(u, "fm"), ACT.Exp, scale=-1.0))
                settle(act.activation(dst, dst, ACT.Ln, bias=ones[:, 0:1]))
                act.activation(dst, dst, ACT.Exp, scale=-1.0).then_inc(silu_sig, 1)

            def qk_rs(n_ss, count):
                act.wait_ge(ss_set, n_ss)
                settle(act.activation(rs[:, 0:count], ss[:, 0:count], ACT.Ln, bias=epsc[:, :], scale=1.0 / HD))
                act.activation(rs[:, 0:count], rs[:, 0:count], ACT.Exp, scale=-0.5).then_inc(rs_set, 1)

            def hg_exps(i):
                if i // 2 < LEVELS:
                    act.wait_ge(hg_arg, i + 1)
                    e = E[:, i % 2, :].rearrange("p (a b) -> p a b", a=2)[:, :, 0:768]
                    act.activation(e, e, ACT.Exp).then_inc(hg_exp, 1)

            def swa(s):
                if s >= 1:
                    b = s - 1
                    nk = P if b // 4 == 0 else NTOK
                    for hh in range(2):
                        full("tb", f"swaP{b}.{hh}")
                        act.activation(PT[:, NTOK * hh:NTOK * hh + nk], TB[:, 0:nk], ACT.Copy).then_inc(tb_free, 1)
                if s < N_SWA:
                    nk = P if s // 4 == 0 else NTOK
                    act.wait_ge(negm_set, s + 1)
                    for hh in range(2):
                        ins = act.activation(PB[:, NTOK * hh:NTOK * hh + nk], SC[:, 512 * hh:512 * hh + nk], ACT.Exp,
                                             bias=negm[:, hh:hh + 1], scale=HD ** -0.5, accum_out=ssum[:, hh:hh + 1])
                    ins.then_inc(sc_free, 1)
                    act.activation(esink, dsink, ACT.Exp).then_inc(exp_set, 1)
                if s >= 1:
                    b = s - 1
                    full("ob", f"swaO{b}")
                    act.activation(obuf[:, b % 4, P * (b // 4):P * (b // 4) + P], OB[:, 0:P], ACT.Copy).then_inc(ob_free, 1)

            def tile():
                act.wait_ge(tile_arg, 1)
                full("sc", "hg15")
                Xf = X[:, 0, :, :].rearrange("p (h s) n -> p h s n", h=H_A)
                Xb = X[:, 1, :, :].rearrange("p (h s) n -> p h s n", h=H_A)

                def part(e, n):
                    return E[:, e, 1024 * n:1024 * n + 1024].rearrange("p (h s n) -> p h s n", h=H_A, s=2)
                act.activation(part(0, 0), Xf[:, :, 1:3, 1:129], ACT.Exp)
                act.activation(part(0, 1), part(0, 1), ACT.Exp)
                act.activation(part(1, 0), part(1, 0), ACT.Exp)
                act.activation(part(1, 1), Xb[:, :, 0:3:2, 0:P], ACT.Exp)
                act.activation(tot[:, 0, :], Xf[:, :, 1, P], ACT.Exp)
                act.activation(tot[:, 1, :], Xb[:, :, 2, P], ACT.Exp).then_inc(tile_exp, 1)
                full("sc", "att8")
                act.activation(kk[:, 0, 0:8, :].rearrange("p a b -> p (a b)"), SC[:, :], ACT.Copy).then_inc(sc_free, 1)
                for d, name in enumerate(("kf_turned", "kb_turned")):
                    full("tb", name)
                    act.activation(kk[:, 1, 4 * d:4 * d + 4, :].rearrange("p a b -> p (a b)"), TB[:, :],
                                   ACT.Copy).then_inc(tb_free, 1)
                for d, name in enumerate(("state_f", "state_b")):
                    full("ob", name)
                    act.activation(X[:, 1, 4 * d:4 * d + 4, 0:P], OB[:, :].rearrange("p (a b) -> p a b", a=4),
                                   ACT.Copy).then_inc(ob_free, 1)
                act.wait_ge(ob_free, OB_USE["state_b"] + 1)
                act.dma_start(t["new_state_hgrn"][0, 0].rearrange("d h k v -> k (d h) v"),
                              X[:, 1, 0:8, 0:P]).then_inc(out_dma, 16)

            def even_jobs(jobs):
                for name in jobs:
                    kind, i = job(name)
                    if kind == "hg":
                        hg_exps(i + 1)
                    elif kind == "swa":
                        swa(i)
                    elif kind == "tq":
                        for j in range(4):
                            full("tb", f"tq{j}")
                            act.activation(qT[:, j, :], TB[:, 0:NTOK], ACT.Copy).then_inc(tb_free, 1)
                        full("tb", "tk")
                        act.activation(kT[:, :], TB[:, :], ACT.Copy).then_inc(tb_free, 1)
                        act.dma_start(t["new_k_swa"][0, 0].rearrange("s n d -> s (n d)"), kout[:, 0, :]).then_inc(out_dma, 16)
                        act.dma_start(t["new_v_swa"][0, 0].rearrange("s n d -> s (n d)"), vout[:, 0, :]).then_inc(out_dma, 16)
                    else:
                        tile()

            def head_read(name, dst, sq, pos_ro):
                full("ob", name)
                act.activation(dst, OB[:, 0:NTOK], ACT.Copy)
                act.activation(sq, OB[:, 0:NTOK], ACT.Square).then_inc(ob_free, 1)

            def head_rstd(name, n):
                full("tb", name)
                if n:
                    act.wait_ge(ro_set, n)
                act.activation(rstd[:, :], TB[:, 0:NTOK], ACT.Ln, bias=epsc[:, :], scale=1.0 / P).then_inc(tb_free, 1)
                act.wait_ge(tb_free, TB_USE[name] + 1)
                act.activation(rstd[:, :], rstd[:, :], ACT.Exp, scale=-0.5).then_inc(ro_rstd, 1)

            for u in range(13):
                ada_copy(OB_USE[f"ada{8 + u}"])
                even_jobs(EVEN_SIDE.get((u, 0), []))
                if u in (1, 2, 3, 4):
                    log_gates(u - 1)
                if u in Z_F + Z_B:
                    gates(u)
                elif u in Q_A:
                    silu_part(hq[:, 6 * (u - 4):6 * (u - 4) + 6, :].rearrange("p a b -> p (a b)"), u)
                elif u in GATE:
                    full("tb", "tq3")
                    i = u - GATE[0]
                    silu_part(qout[:, :, :].rearrange("p a b -> p (a b)")[:, 768 * i:768 * i + 768], u)
                elif u in V_A:
                    i = u - V_A[0]
                    act.activation(vtok[:, :, UC * i:UC * i + UC], unit_out(u, "tok").rearrange("p (a b) -> p a b", a=TT),
                                   ACT.Copy).then_inc(g_free[u % 2], 1)
                elif u in Q_SWA:
                    if u > Q_SWA[0]:
                        act.wait_ge(rope_set, u - Q_SWA[0])
                    act.activation(PT[:, 0:768], unit_out(u, "tok"), ACT.Square)
                    act.activation(PB[:, 0:768], unit_out(u, "tok"), ACT.Copy).then_inc(g_free[u % 2], 1)
                else:
                    act.wait_ge(rope_set, 2)
                    g3 = unit_out(u, "tok").rearrange("p (a b) -> p a b", a=TT)
                    act.activation(PT[:, 0:NTOK].rearrange("p (a b) -> p a b", a=TT), g3[:, :, 0:P], ACT.Square)
                    act.activation(PB[:, 0:NTOK].rearrange("p (a b) -> p a b", a=TT), g3[:, :, 0:P], ACT.Copy)
                    act.activation(vout[:, :, :], g3[:, :, P:UC], ACT.Copy).then_inc(g_free[u % 2], 1)
                split(u + 2)
                if u in Q_SWA + KV_SWA:
                    qk_rs(u - Q_SWA[0] + 1, 12 if u in Q_SWA else 6)
                if u == 5:
                    hg_exps(0)
                even_jobs(EVEN_SIDE.get((u, 1), []))
            even_jobs(EVEN_TAIL)
            act.wait_ge(ob_free, OB_USE[f"swaO{N_SWA - 1}"] + 1)
            for n in range(4):
                act.activation(opH[:, 4 + n, :], obuf[:, n, :], ACT.Copy).then_inc(oph_set, 1)
            for h in range(H_A + 1):
                if h < H_A:
                    head_read(f"hgO{h}", hq[:, 3 * h:3 * h + 3, :].rearrange("p a b -> p (a b)"), nbuf[:, h % 2, :], h)
                if h:
                    head_rstd(f"hgN{h - 1}", h - 1)
            for h in range(H_A):
                act.wait_ge(ro_set, h + 1)
                act.activation(opH[:, h, :], hq[:, 3 * h:3 * h + 3, :].rearrange("p a b -> p (a b)"),
                               ACT.Copy).then_inc(oph_set, 1)
            for u in range(13, 17):
                if u < 16:
                    ada_copy(OB_USE[f"ada{8 + u}"])
                act.wait_ge(gemm_done, u + 1)
                if u < 16:
                    split(u + 2)

            def added(base):
                def wait(k):
                    u = base + k // 2
                    act.wait_ge(g_free[u % 2], u // 2 + 1)
                return wait

            norm(1, added(U_OUT_E))
            shift(1, 2 * KT)

            def mlp_group(base, g, pos, per, n_hid, with_ada, last):
                gap = 2 if per == 16 else 1
                for i in range(8):
                    u = base + i
                    if with_ada:
                        ada_copy(OB_USE["ada24"] + i, g)
                    if i == 0:
                        split_high(u + 1, pos + gap, g, per)
                    if i < 4:
                        act.wait_ge(gemm_done, u + 1 + 8 * g)
                        if i >= 2:
                            act.wait_ge(relu2_set, n_hid + i - 1 + 4 * g)
                        r = relu[:, u % 2, :]
                        act.activation(r.rearrange("p (m n) -> p m n", m=2),
                                       G[:, u % 2, :].rearrange("p (m n) -> p m n", m=2)[:, :, 0:NTOK],
                                       ACT.Relu).then_inc(g_free[u % 2], 1)
                        act.wait_ge(g_free[u % 2], (u // 2 + 1) + 4 * g)
                        act.activation(hidH[:, 2 * i:2 * i + 2, :].rearrange("p a b -> p (a b)"), r,
                                       ACT.Square).then_inc(relu_sq, 1)
                    if i <= 5 or (i == 6 and not last):
                        nxt = pos + gap * (i + 2)
                        split_high(u + 2, nxt, g, per)

            act.wait_ge(out_dma, 16 * 3)
            b0, b1 = POS["u", U_MLP0], POS["u", U_MLP1]
            with act.Fori(0, 3) as g:
                mlp_group(U_MLP0, g, b0, 16, 0, True, False)
            mlp_group(U_MLP0 + 24, 0, b0 + 48, 8, 12, False, False)
            split(U_ODD + 1)
            norm(2, added(U_MLP0 + 28))
            shift(2, 3 * KT)

            act.wait_ge(lamr_set, 1)
            act.activation(lam2, lam2, ACT.Exp).then_inc(lam_exp, 1)

            def diff(s):
                if s >= 1:
                    b = s - 1
                    nk = P if b % 3 == 0 else NTOK
                    full("tb", f"dP{b}")
                    act.activation(DPT[:, 0:nk], TB[:, 0:nk], ACT.Copy).then_inc(tb_free, 1)
                if s < N_DIFF:
                    nk = P if s % 3 == 0 else NTOK
                    act.wait_ge(dnegm_set, s + 1)
                    for c in range(2):
                        ins = act.activation(DP[:, c, 0:nk], SC[:, 512 * c:512 * c + nk], ACT.Exp,
                                             bias=negm[:, c:c + 1], scale=HD ** -0.5, accum_out=ssum[:, c:c + 1])
                    ins.then_inc(sc_free, 1)
                if s >= 1 and (s - 1) % 3 == 2:
                    h = (s - 1) // 3
                    head_read(f"dO{h}", doT[:, h, :], nbuf[:, h % 2, :], h)
                    head_rstd(f"dN{h}", H_A + h)

            for u in range(12):
                for s in odd_slots(u, 0):
                    diff(s)
                g = unit_out(U_ODD + u, "tok")
                part, j = u % 3, u // 3
                if part < 2:
                    if u:
                        act.wait_ge(rope_set, 3 + 2 * j + part)
                    act.activation(dsq[:, :], g, ACT.Square)
                    act.activation(draw[:, :], g, ACT.Copy).then_inc(g_free[(U_ODD + u) % 2], 1)
                else:
                    act.activation(dv[:, :, UC * j:UC * j + UC], g.rearrange("p (a b) -> p a b", a=TT),
                                   ACT.Copy).then_inc(g_free[(U_ODD + u) % 2], 1)
                split(U_ODD + u + 2)
                if part < 2:
                    qk_rs(3 + 2 * j + part + 1, 12)
                for s in odd_slots(u, 1):
                    diff(s)
                for name in odd_turns(u):
                    full("tb", name)
                    if name.startswith("kc"):
                        n = int(name[2])
                        act.activation(dkT[:, 4 * n:4 * n + 4, NTOK:512], TB[:, :].rearrange("p (a b) -> p a b", a=4),
                                       ACT.Copy).then_inc(tb_free, 1)
                    else:
                        dst = (dqT, dkT)[(u - 1) % 3]
                        act.activation(dst[:, 2 * ((u - 1) // 3) + int(name[-1]), 0:NTOK], TB[:, 0:NTOK],
                                       ACT.Copy).then_inc(tb_free, 1)
            act.wait_ge(g_free[(U_ODD + 11) % 2], (U_ODD + 11) // 2 + 1)
            act.dma_start(t["new_v_diff"][0, 0].rearrange("s h e -> s (h e)"), dv[:, 0, :]).then_inc(out_dma, 16)
            for s in odd_slots(12, 0):
                diff(s)
            for h in range(H_C):
                act.wait_ge(ro_set, H_A + h + 1)
                act.activation(opH[:, h, :], doT[:, h, :], ACT.Copy).then_inc(oph_set, 1)
            for u in range(4):
                act.wait_ge(gemm_done, U_OUT_O + u + 1)
                if u < 3:
                    split(U_OUT_O + u + 2)
            norm(3, added(U_OUT_O))
            shift(3, 5 * KT)
            act.wait_ge(out_dma, 16 * 4)
            act.wait_ge(kd_out, 16 * 4)
            with act.Fori(0, 3) as g:
                mlp_group(U_MLP1, g, b1, 8, 16, False, False)
            mlp_group(U_MLP1 + 24, 0, b1 + 24, 8, 28, False, True)
            for n in range(6):
                full("tb", f"y{n}")
                act.activation(yout[:, n // 2, 512 * (n % 2):512 * (n % 2) + 512], TB[:, :], ACT.Copy).then_inc(tb_free, 1)

        @block.vector
        def _(dve):
            steps = [0]

            def settle(ins):
                steps[0] += 1
                ins.then_inc(dve_step, 1)
                dve.wait_ge(dve_step, steps[0])

            def full(buf, name):
                uses, filled = {"sc": (SC_USE, sc_full), "tb": (TB_USE, tb_full)}[buf]
                dve.wait_ge(filled, uses[name] + 1)

            def split_low(u, g=0, pos=None):
                pos = POS["u", u] if pos is None else pos
                dve.wait_ge(w_high, u + 1 + 8 * g)
                dve.tensor_tensor(wL[:, u % 2, :, :], raw[:, pos % RAW, :, :], wH[:, u % 2, :, :].bitcast(F32),
                                  ALU.subtract).then_inc(w_split, 1)

            def ada_mods(layer, pair, n_tb, n_set, g=0):
                dve.wait_ge(tb_full, n_tb + 1 + 8 * g)
                if not isinstance(n_set, int) or n_set:
                    dve.wait_ge(mods_set, n_set)
                src = TB[:, 0:UC].rearrange("p (i g c) -> p i c g", i=2, g=4)[:, :, 0:2, :]
                dve.tensor_reduce(adat, src, AX.X, ALU.add).then_inc(tb_free, 1)
                dve.wait_ge(tb_free, n_tb + 1 + 8 * g)
                out = mods[:, layer, pair, :]
                b = bada[:, layer, pair].rearrange("p (i o) -> p i o", o=1).broadcast_to([P, 2, 2])
                dve.tensor_tensor(out, adat, b, ALU.add).then_inc(mods_set, 1)

            def ada(a):
                j = 2 * (a % ADA_COLS)
                ada_mods(a // ADA_COLS, slice(j, j + 2), TB_USE[f"ada{a}"], a)

            def scales(n, n_mods):
                dve.wait_ge(mods_set, n_mods)
                part = SC1 if n % 2 == 0 else SC2
                sc = mods[:, n // 2, KT * part:KT * part + KT, :]
                w = normw[:, n, :].rearrange("p (t o) -> p t o", o=1).broadcast_to([P, KT, 2])
                settle(dve.scalar_tensor_tensor(scale1[:, n, :, :], sc, 1.0, w, ALU.add, ALU.mult))

            def modulate(n, n_op):
                part = SH1 if n % 2 == 0 else SH2
                spans = ((0, P), (P, NTOK))
                dve.wait_ge(rstd_set, n + 1)
                for k in range(KT + 1):
                    if k < KT:
                        if k >= 2:
                            dve.wait_ge(op_set, n_op + k - 1)
                        for c, (a, b) in enumerate(spans):
                            ins = dve.scalar_tensor_tensor(nbuf[:, k % 2, a:b], xT[:, k, a:b],
                                                           scale1[:, n, k, c:c + 1], rstd[:, a:b], ALU.mult, ALU.mult)
                        ins.then_inc(scaled_set, 1)
                    if k:
                        q = k - 1
                        dve.wait_ge(oph_set, n_op + q + 1)
                        dve.wait_ge(scaled_set, KT * n + q + 1)
                        for c, (a, b) in enumerate(spans):
                            ins = dve.scalar_tensor_tensor(opL[:, q, a:b], nbuf[:, q % 2, a:b],
                                                           mods[:, n // 2, KT * part + q, c:c + 1],
                                                           opH[:, q, a:b].bitcast(F32), ALU.add, ALU.subtract)
                        ins.then_inc(op_set, 1)

            def residual(u, gate, layer, tile0, g=0):
                dve.wait_ge(gemm_done, u + 1 + 8 * g)
                for m in range(2):
                    k = tile0 + m
                    for c, (a, b) in enumerate(((0, P), (P, NTOK))):
                        ins = dve.scalar_tensor_tensor(xT[:, k, a:b], G[:, u % 2, 512 * m + a:512 * m + b],
                                                       mods[:, layer, KT * gate + k, c:c + 1], xT[:, k, a:b],
                                                       ALU.mult, ALU.add)
                ins.then_inc(g_free[u % 2], 1)

            dve.wait_ge(cexp_set, 1)
            settle(dve.tensor_scalar(sgt, sgt, 1.0, None, ALU.add))
            settle(dve.reciprocal(sgt, sgt))
            dve.wait_ge(cst_zero, 1)
            dve.tensor_tensor(cst[:, :, 0:2].rearrange("p t c -> p c t"), c2, sgt.rearrange("p (c t) -> p c t", c=2),
                              ALU.mult).then_inc(cst_set, 1)
            dve.tensor_tensor(lb, lbl, lbl, ALU.subtract).then_inc(lbmax_sub, 1)
            dve.wait_ge(cexp_set, 2)
            settle(dve.reciprocal(omlb, lb))
            settle(dve.tensor_tensor(omlb, lb, omlb, ALU.mult))
            settle(dve.tensor_tensor(lb, omlb, omlb, ALU.subtract))
            settle(dve.tensor_scalar(omlb, lb, -1.0, 1.0, ALU.mult, ALU.add))
            dve.tensor_scalar(subs, subw, 1.0 - LAM_INIT, None, ALU.mult)
            for a in range(8):
                ada(a)
            split_low(0)
            split_low(1)
            scales(0, 8)
            modulate(0, 0)

            def forget(u):
                d, i = u // 2, u % 2
                dve.wait_ge(sig_set, u + 1)
                for m in range(2):
                    h = 4 * d + 2 * i + m
                    s = E[:, i, NTOK * m:NTOK * m + NTOK]
                    ins = dve.tensor_scalar(s, s, omlb[:, h:h + 1], lb[:, h:h + 1], ALU.mult, ALU.add)
                ins.then_inc(f_set, 1)

            def scans(u):
                d, i = u // 2, u % 2
                dve.wait_ge(logf_set, u + 1)
                for m in range(6):
                    ins = dve.tensor_tensor_scan(X[:, d, 6 * i + m, 1:129], ones[:, :],
                                                 E[:, i, 1024 + P * m:1024 + P * m + P], 0.0, ALU.mult, ALU.add)
                ins.then_inc(scans_done, 1)

            def silu_mul(dst, u, n, scale):
                dve.wait_ge(silu_sig, n)
                g = G[:, u % 2, :].rearrange("p (m n) -> p m n", m=2)[:, :, 0:NTOK]
                d = dst.rearrange("p (m n) -> p m n", m=2)
                dve.scalar_tensor_tensor(d, g, scale, d, ALU.mult, ALU.mult).then_inc(g_free[u % 2], 1)

            def qk_norm(raw3, sq, u, n, count):
                dve.wait_ge(g_free[u % 2], u // 2 + 1)
                dve.tensor_reduce(ss[:, 0:count], sq.rearrange("p (a b) -> p a b", b=HD), AX.X, ALU.add).then_inc(ss_set, 1)

            def qk_scale(raw3, n, count):
                dve.wait_ge(rs_set, n)
                x3 = raw3.rearrange("p (a b) -> p a b", b=HD)
                dve.tensor_tensor(x3, x3, rs[:, 0:count].rearrange("p (a o) -> p a o", o=1).broadcast_to([P, count, HD]),
                                  ALU.mult).then_inc(xr_set, 1)

            def hg_muls(i):
                grp, lev = i % 2, i // 2
                if i >= N_HG:
                    return
                if i == 0:
                    dve.wait_ge(k_set, 4)
                if lev == LEVELS:
                    full("sc", f"hg{i - 2}")
                    dve.tensor_tensor(E[:, grp, 1024:1792], kk[:, 0, 6 * grp:6 * grp + 6, :].rearrange("p a b -> p (a b)"),
                                      kk[:, 1, 6 * grp:6 * grp + 6, :].rearrange("p a b -> p (a b)"),
                                      ALU.add).then_inc(hg_mul, 1)
                    return
                dve.wait_ge(hg_exp, i + 1)
                hf = 2 ** lev
                q = E[:, grp, 0:768]
                dve.tensor_tensor(q, q, hq[:, 6 * grp:6 * grp + 6, :].rearrange("p a b -> p (a b)"), ALU.mult)
                ek = E[:, grp, 1024:1792].rearrange("p (c h j) -> p c h j", h=2, j=hf)
                for d in range(2):
                    src = kk[:, d, 6 * grp:6 * grp + 6, :].rearrange("p a (c h j) -> p (a c) h j", h=2, j=hf)
                    ins = dve.tensor_tensor(ek[:, :, d, :], ek[:, :, d, :], src[:, :, d, :], ALU.mult)
                ins.then_inc(hg_mul, 1)

            def hg_pick(i):
                grp, lev = i % 2, i // 2
                full("sc", f"hg{i}")
                dve.copy_predicated(att[:, 6 * grp:6 * grp + 6, :],
                                    masks[:, lev:lev + 1, :].broadcast_to([P, 6, P]),
                                    SC[:, 0:768].rearrange("p (a b) -> p a b", a=6)).then_inc(sc_free, 1)

            def swa(s):
                if s >= 1:
                    b = s - 1
                    nk = P if b // 4 == 0 else NTOK
                    dve.wait_ge(exp_set, s)
                    settle(dve.tensor_tensor(den, ssum, esink, ALU.add))
                    settle(dve.reciprocal(rden, den))
                    for hh in range(2):
                        p = PB[:, NTOK * hh:NTOK * hh + nk]
                        ins = dve.tensor_scalar(p, p, rden[:, hh:hh + 1], None, ALU.mult)
                    ins.then_inc(p_set, 1)
                if s < N_SWA:
                    ti, pair = s // 4, s % 4
                    nk = P if ti == 0 else NTOK
                    sk = sinkb[:, 2 * pair:2 * pair + 2]
                    full("sc", f"swa{s}")
                    settle(dve.tensor_reduce(mx, SC[:, :].rearrange("p (a b) -> p a b", a=2)[:, :, 0:nk], AX.X, ALU.max))
                    settle(dve.scalar_tensor_tensor(mx, mx, HD ** -0.5, sk, ALU.mult, ALU.max))
                    dve.tensor_tensor(dsink, sk, mx, ALU.subtract)
                    dve.tensor_scalar(negm, mx, -1.0, None, ALU.mult).then_inc(negm_set, 1)

            def tile():
                dve.wait_ge(tile_exp, 1)
                q4 = hq[:, :, :].rearrange("p (h s) n -> p h s n", h=H_A)
                kf = kk[:, 0, :, :].rearrange("p (h s) n -> p h s n", h=H_A)
                kb = kk[:, 1, :, :].rearrange("p (h s) n -> p h s n", h=H_A)
                for e, n, src in ((0, 0, q4[:, :, 1:3, :]), (0, 1, q4[:, :, 1:3, :]),
                                  (1, 0, kf[:, :, 0:2, :]), (1, 1, kb[:, :, 0:3:2, :])):
                    x = E[:, e, 1024 * n:1024 * n + 1024].rearrange("p (h s n) -> p h s n", h=H_A, s=2)
                    ins = dve.tensor_tensor(x, x, src, ALU.mult)
                ins.then_inc(tile_mul, 1)
                for d in range(2):
                    w = tot[:, d, :].rearrange("p (h o) -> p h o", o=1).broadcast_to([P, H_A, P])
                    ins = dve.tensor_tensor(X[:, 0, 4 * d:4 * d + 4, 0:P], S0[:, d, :, :], w, ALU.mult)
                ins.then_inc(s0_set, 1)

            def even_jobs(jobs):
                for name in jobs:
                    kind, i = job(name)
                    if kind == "hg":
                        hg_muls(i + 1)
                        hg_pick(i)
                    elif kind == "swa":
                        swa(i)
                    elif kind == "tile":
                        tile()

            def low_part(k, src, n_oph):
                dve.wait_ge(oph_set, n_oph)
                dve.tensor_tensor(opL[:, k, :], src, opH[:, k, :].bitcast(F32), ALU.subtract).then_inc(op_set, 1)

            for u in range(13):
                even_jobs(EVEN_SIDE.get((u, 0), []))
                if u in (1, 2, 3, 4):
                    scans(u - 1)
                if u in Z_F + Z_B:
                    forget(u)
                elif u in Q_A:
                    silu_mul(hq[:, 6 * (u - 4):6 * (u - 4) + 6, :].rearrange("p a b -> p (a b)"), u, u - 3, P ** -0.5)
                elif u in GATE:
                    i = u - GATE[0]
                    silu_mul(qout[:, :, :].rearrange("p a b -> p (a b)")[:, 768 * i:768 * i + 768], u, 3 + i, 1.0)
                elif u in Q_SWA + KV_SWA:
                    count = 12 if u in Q_SWA else 6
                    qk_norm(PB, PT[:, 0:HD * count], u, u - 5, count)
                split_low(u + 2)
                if u in Q_SWA + KV_SWA:
                    count = 12 if u in Q_SWA else 6
                    qk_scale(PB[:, 0:HD * count], u - 5, count)
                if u == 5:
                    hg_muls(0)
                even_jobs(EVEN_SIDE.get((u, 1), []))
                ada(8 + u)
            even_jobs(EVEN_TAIL)
            for n in range(4):
                low_part(4 + n, obuf[:, n, :], KT + n + 1)

            def head_scale(n, x, w, gate):
                dve.wait_ge(ro_rstd, n + 1)
                if gate is None:
                    dve.scalar_tensor_tensor(x, x, w, rstd[:, :], ALU.mult, ALU.mult).then_inc(ro_set, 1)
                else:
                    settle(dve.scalar_tensor_tensor(x, x, w, rstd[:, :], ALU.mult, ALU.mult))
                    dve.tensor_tensor(x, x, gate, ALU.mult).then_inc(ro_set, 1)

            gate_all = qout[:, :, :].rearrange("p a b -> p (a b)")
            dve.wait_ge(g_free[1], 6)
            dve.wait_ge(g_free[0], 7)
            for h in range(H_A):
                head_scale(h, hq[:, 3 * h:3 * h + 3, :].rearrange("p a b -> p (a b)"), hgw,
                           gate_all[:, NTOK * h:NTOK * h + NTOK])
            for h in range(H_A):
                low_part(h, hq[:, 3 * h:3 * h + 3, :].rearrange("p a b -> p (a b)"), KT + 4 + h + 1)
            for u in range(13, 17):
                dve.wait_ge(mods_set, 20)
                residual(u, G1, 0, 2 * (u - 13))
                if u < 16:
                    split_low(u + 2)
                    ada(8 + u)
            scales(1, 20)
            modulate(1, 2 * KT)

            def mlp_group(layer, base, g, pos, per, n_hid, with_ada, last):
                gap = 2 if per == 16 else 1
                for i in range(8):
                    u = base + i
                    if i == 0:
                        split_low(u + 1, g, pos + gap)
                    if i < 4:
                        dve.wait_ge(relu2_set, n_hid + i + 1 + 4 * g)
                        dve.wait_ge(relu_sq, n_hid + i + 1 + 4 * g)
                        dve.tensor_tensor(hidL[:, 2 * i:2 * i + 2, :].rearrange("p a b -> p (a b)"), relu2[:, u % 2, :],
                                          hidH[:, 2 * i:2 * i + 2, :].rearrange("p a b -> p (a b)").bitcast(F32),
                                          ALU.subtract).then_inc(hid_set, 1)
                    else:
                        residual(u, G2, layer, 2 * (i - 4), g)
                    if i <= 5 or (i == 6 and not last):
                        split_low(u + 2, g, pos + gap * (i + 2))
                    if with_ada:
                        ada_mods(1, bass.ds(2 * i + 16 * g, 2), TB_USE["ada24"] + i, 24 + i + 8 * g, g)

            b0, b1 = POS["u", U_MLP0], POS["u", U_MLP1]
            dve.wait_ge(mods_set, 24)
            with dve.Fori(0, 3) as g:
                mlp_group(0, U_MLP0, g, b0, 16, 0, True, False)
            mlp_group(0, U_MLP0 + 24, 0, b0 + 48, 8, 12, False, False)
            split_low(U_ODD + 1)
            scales(2, 48)
            modulate(2, 3 * KT)

            dve.wait_ge(odd_in, 16 * 3)
            for n in range(2):
                settle(dve.tensor_tensor(lamp[:, 2 * n, :], lamp[:, 2 * n, :], lamp[:, 2 * n + 1, :], ALU.mult))
            dve.tensor_reduce(lam2, lamp[:, 0:4:2, :], AX.X, ALU.add).then_inc(lamr_set, 1)
            dve.wait_ge(lam_exp, 1)
            settle(dve.scalar_tensor_tensor(lam, lam2[:, 1:2], LAM_INIT, lam2[:, 0:1], ALU.subtract, ALU.subtract))

            def diff(s):
                if s >= 1:
                    b = s - 1
                    nk = P if b % 3 == 0 else NTOK
                    dve.wait_ge(sc_free, SC_USE[f"d{b}"] + 1)
                    settle(dve.reciprocal(rden, ssum))
                    settle(dve.tensor_tensor(rden[:, 1:2], rden[:, 1:2], lam, ALU.mult))
                    settle(dve.tensor_scalar(DW[:, 0:nk], DP[:, 1, 0:nk], rden[:, 1:2], None, ALU.mult))
                    dve.scalar_tensor_tensor(DW[:, 0:nk], DP[:, 0, 0:nk], rden[:, 0:1], DW[:, 0:nk], ALU.mult,
                                             ALU.add).then_inc(dw_set, 1)
                if s < N_DIFF:
                    nk = P if s % 3 == 0 else NTOK
                    full("sc", f"d{s}")
                    settle(dve.tensor_reduce(mx, SC[:, :].rearrange("p (a b) -> p a b", a=2)[:, :, 0:nk], AX.X, ALU.max))
                    dve.tensor_scalar(negm, mx, -HD ** -0.5, None, ALU.mult).then_inc(dnegm_set, 1)
                if s >= 1 and (s - 1) % 3 == 2:
                    h = (s - 1) // 3
                    head_scale(H_A + h, doT[:, h, :], subs, None)

            for u in range(12):
                part, j = u % 3, u // 3
                for s in odd_slots(u, 0):
                    diff(s)
                if part < 2:
                    qk_norm(draw, dsq[:, :], U_ODD + u, 3 + 2 * j + part + 1, 12)
                else:
                    dve.wait_ge(g_free[(U_ODD + u) % 2], (U_ODD + u) // 2 + 1)
                split_low(U_ODD + u + 2)
                if part < 2:
                    qk_scale(draw[:, :], 3 + 2 * j + part + 1, 12)
                for s in odd_slots(u, 1):
                    diff(s)
            for s in odd_slots(12, 0):
                diff(s)
            for h in range(H_C):
                low_part(h, doT[:, h, :], 4 * KT + h + 1)
            for u in range(4):
                residual(U_OUT_O + u, G1, 1, 2 * u)
                if u < 3:
                    split_low(U_OUT_O + u + 2)
            scales(3, 48)
            modulate(3, 5 * KT)
            with dve.Fori(0, 3) as g:
                mlp_group(1, U_MLP1, g, b1, 8, 16, False, False)
            mlp_group(1, U_MLP1 + 24, 0, b1 + 24, 8, 28, False, True)

        @block.gpsimd
        def _(pool):
            steps = [0]

            def settle(ins):
                steps[0] += 1
                ins.then_inc(pool_step, 1)
                pool.wait_ge(pool_step, steps[0])

            pool.memset(epsc[:, :], EPS)
            pool.memset(ones[:, :], 1.0).then_inc(ones_set, 1)
            pool.memset(cst[:, :, :], 0.0).then_inc(cst_zero, 1)
            pool.wait_ge(even_in, 16 * 12)

            def tables(dst, w0):
                for n in range(2):
                    for cs in range(2):
                        w = wrow[:, w0 + n:w0 + n + 1, :].broadcast_to([P, 2, HD])
                        ins = pool.tensor_tensor(dst[:, n, cs, :, :], trig[:, cs, :, :], w, ALU.mult)
                return ins

            settle(tables(ropeE, 0))
            pool.wait_ge(tb_full, TB_USE[f"x{KT - 1}"] + 1)
            settle(pool.memset(X[:, :, :, 0:1], 0.0))

            def keys(u):
                d, i = u // 2, u % 2
                pool.wait_ge(f_set, u + 1)
                pool.tensor_scalar(kk[:, d, 6 * i:6 * i + 6, :].rearrange("p a b -> p (a b)"), E[:, i, 0:768], -1.0, 1.0,
                                   ALU.mult, ALU.add).then_inc(k_set, 1)

            def hg_args(i):
                grp, lev = i % 2, i // 2
                if lev >= LEVELS:
                    return
                if i == 0:
                    pool.wait_ge(scans_done, 4)
                    pool.wait_ge(k_set, 4)
                if i >= 2:
                    pool.wait_ge(sc_full, SC_USE[f"hg{i - 2}"] + 1)
                hf = 2 ** lev
                nb = P // (2 * hf)

                def halves(d, off):
                    x = X[:, d, 6 * grp:6 * grp + 6, off:off + P]
                    return x.rearrange("p a (c h j) -> p a c h j", h=2, j=hf)

                def mid(d):
                    return halves(d, 0)[:, :, :, 1, 0:1].broadcast_to([P, 6, nb, hf])

                q = E[:, grp, 0:768].rearrange("p (a c h j) -> p a c h j", a=6, h=2, j=hf)
                k = E[:, grp, 1024:1792].rearrange("p (a c h j) -> p a c h j", a=6, h=2, j=hf)
                pool.tensor_tensor(q[:, :, :, 1, :], halves(0, 1)[:, :, :, 1, :], mid(0), ALU.subtract)
                pool.tensor_tensor(k[:, :, :, 0, :], mid(0), halves(0, 1)[:, :, :, 0, :], ALU.subtract)
                pool.tensor_tensor(q[:, :, :, 0, :], mid(1), halves(1, 0)[:, :, :, 0, :], ALU.subtract)
                pool.tensor_tensor(k[:, :, :, 1, :], halves(1, 0)[:, :, :, 1, :], mid(1),
                                   ALU.subtract).then_inc(hg_arg, 1)

            def rope(x, tmp, tab, w, out, heads):
                c, s = (tab[:, n, :, :].rearrange("p t (o d) -> p t o d", o=1).broadcast_to([P, 2, heads, HD])
                        for n in range(2))
                pool.tensor_tensor(out[:, 0], x[:, 0], w.broadcast_to([P, heads, HD]), ALU.mult)
                pool.tensor_tensor(tmp, x[:, 1:3], s, ALU.mult)
                settle(pool.tensor_tensor(out[:, 1:3], x[:, 1:3], c, ALU.mult))
                for tt in range(2):
                    for o in range(2):
                        ins = pool.tensor_tensor(out[:, 1 + tt, :, o::2], out[:, 1 + tt, :, o::2],
                                                 tmp[:, tt, :, 1 - o::2], ALU.add)
                return ins

            def even_unit_rope(u):
                n = u - Q_SWA[0]
                pool.wait_ge(xr_set, n + 1)
                heads = 4 if u in Q_SWA else 2
                x = PB[:, 0:3 * HD * heads].rearrange("p (t h d) -> p t h d", t=TT, d=HD)
                tmp = PT[:, 0:2 * HD * heads].rearrange("p (t h d) -> p t h d", t=2, d=HD)
                if u in Q_SWA:
                    out = qout[:, :, :].rearrange("p t (h o d) -> p t h o d", o=2, d=HD)[:, :, :, n, :]
                else:
                    out = kout[:, :, :].rearrange("p t (h d) -> p t h d", d=HD)
                qk = 0 if u in Q_SWA else 1
                rope(x, tmp, ropeE[:, qk], wrow[:, qk:qk + 1, :], out, heads).then_inc(rope_set, 1)

            def tile_args():
                pool.wait_ge(sc_full, SC_USE["hg15"] + 1)
                Xf = X[:, 0, :, :].rearrange("p (h s) n -> p h s n", h=H_A)
                Xb = X[:, 1, :, :].rearrange("p (h s) n -> p h s n", h=H_A)
                qb = E[:, 0, 1024:2048].rearrange("p (h s n) -> p h s n", h=H_A, s=2)
                kf = E[:, 1, 0:1024].rearrange("p (h s n) -> p h s n", h=H_A, s=2)
                pool.tensor_tensor(qb, Xb[:, :, 1:3, P:P + 1].broadcast_to([P, H_A, 2, P]), Xb[:, :, 1:3, 0:P], ALU.subtract)
                pool.tensor_tensor(kf, Xf[:, :, 0:2, P:P + 1].broadcast_to([P, H_A, 2, P]), Xf[:, :, 0:2, 1:129],
                                   ALU.subtract).then_inc(tile_arg, 1)

            for u in range(4):
                keys(u)
            hg_args(0)
            hg_args(1)
            for u in range(6, 13):
                if u in Q_SWA + KV_SWA:
                    even_unit_rope(u)
                for half in range(2):
                    for name in EVEN_SIDE.get((u, half), []):
                        kind, i = job(name)
                        if kind == "hg":
                            hg_args(i + 2)
            for name in EVEN_TAIL:
                kind, i = job(name)
                if kind == "hg":
                    hg_args(i + 2)
                elif kind == "tile":
                    tile_args()

            pool.wait_ge(op_set, 2 * KT)
            pool.wait_ge(out_dma, 16 * 3)
            pool.dma_start(dkc[:, :], t["cache_k_diff"][0, 0].rearrange("s h c d -> s (h c d)")).then_inc(odd_in, 16)
            pool.dma_start(dvc[:, :], t["cache_v_diff"][0, 0].rearrange("s h e -> s (h e)")).then_inc(odd_in, 16)
            pool.dma_start(lamp[:, :, :], t["diff_lambda_p"].rearrange("o a d -> o (a d)").broadcast_to([P, 4 * HD])
                           .rearrange("p (a d) -> p a d", a=4)).then_inc(odd_in, 16)
            tables(ropeO, 2).then_inc(rope_tab, 1)

            def relu_squares(base, g, n_hid):
                for i in range(4):
                    u = base + i
                    pool.wait_ge(g_free[u % 2], u // 2 + 1 + 4 * g)
                    if i >= 2:
                        pool.wait_ge(hid_set, n_hid + i - 1 + 4 * g)
                    pool.tensor_tensor(relu2[:, u % 2, :], relu[:, u % 2, :], relu[:, u % 2, :],
                                       ALU.mult).then_inc(relu2_set, 1)

            with pool.Fori(0, 4) as g:
                relu_squares(U_MLP0, g, 0)

            pool.wait_ge(rope_tab, 1)
            for j in range(4):
                for part in range(2):
                    pool.wait_ge(xr_set, 3 + 2 * j + part + 1)
                    if j:
                        pool.wait_ge(tb_full, TB_USE[f"t{3 * (j - 1) + part}.1"] + 1)
                    if j and part:
                        pool.wait_ge(kd_out, 16 * j)
                    x = draw[:, :].rearrange("p (t h d) -> p t h d", t=TT, d=HD)
                    tmp = dsq[:, 0:512].rearrange("p (t h d) -> p t h d", t=2, d=HD)
                    out = dout[:, part, :, :].rearrange("p t (h d) -> p t h d", d=HD)
                    rope(x, tmp, ropeO[:, part], wrow[:, 2 + part:3 + part, :], out, 4).then_inc(rope_set, 1)
                    if part:
                        pool.wait_ge(rope_set, 3 + 2 * (j + 1))
                        pool.dma_start(t["new_k_diff"][0, 0].rearrange("s h c d -> s (h c d)")[:, UC * j:UC * j + UC],
                                       dout[:, 1, 0, :]).then_inc(kd_out, 16)
            pool.wait_ge(out_dma, 16 * 4)
            pool.wait_ge(kd_out, 16 * 4)
            with pool.Fori(0, 4) as g:
                relu_squares(U_MLP1, g, 16)


_INS = ["x_prompt", "x_sample", "cache_k_swa", "cache_v_swa", "state_hgrn", "cache_k_diff", "cache_v_diff",
        "c", "c_ctx", "norm_w", "w_ada", "b_ada", "w_in_even", "w_out_even", "hgrn_lb_logits", "hgrn_norm_w",
        "swa_qnorm_w", "swa_knorm_w", "swa_sink", "w_in_odd", "w_out_odd", "diff_qnorm_w", "diff_knorm_w",
        "diff_lambda_p", "diff_subln_w", "w_mlp1", "w_mlp2"]
_OUTS = [("y_prompt", (1, 128, 1024)), ("y_sample", (1, 256, 1024)), ("new_k_swa", (1, 1, 128, 2, 64)),
         ("new_v_swa", (1, 1, 128, 2, 64)), ("new_state_hgrn", (1, 1, 2, 4, 128, 128)),
         ("new_k_diff", (1, 1, 128, 8, 2, 64)), ("new_v_diff", (1, 1, 128, 8, 128))]


def bf16_words(a):
    return (a.view(np.uint32) >> 16).astype(np.uint16).view(np.int32)


def shape_constants():
    at = np.arange(P)
    masks = np.zeros((P, 8, P), np.uint8)
    for lev in range(LEVELS):
        same_block = (at[:, None] >> (lev + 1)) == (at[None, :] >> (lev + 1))
        other_half = (at[:, None] >> lev) != (at[None, :] >> lev)
        masks[:, lev, :] = same_block & other_half
    masks[:, LEVELS, :] = np.eye(P)
    masks = masks.reshape(P, 8 * P).view(np.int32)
    wmask = np.zeros((P, 2, P), np.float32)
    wmask[:, 0, :][at[None, :] > at[:, None]] = -1e30
    wmask[:, 1, :][at[None, :] < at[:, None]] = -1e30
    pos = np.arange(2 * P)
    row, col = (pos // GRID_W).astype(np.float32), (pos % GRID_W).astype(np.float32)
    half = HD // 2
    inv = (np.float32(10000.0) ** (-np.arange(0, half, 2, dtype=np.float32) / half)).astype(np.float32)
    ang = np.concatenate([row[:, None] * inv, col[:, None] * inv], -1)
    cos, sin = np.cos(ang), np.sin(ang)
    trig = np.zeros((P, 2, 2, HD), np.float32)
    for tt in range(2):
        rows = slice(P * tt, P * tt + P)
        trig[:, 0, tt, 0::2], trig[:, 0, tt, 1::2] = cos[rows], cos[rows]
        trig[:, 1, tt, 0::2], trig[:, 1, tt, 1::2] = sin[rows], -sin[rows]
    return {"ident": np.eye(P, dtype=np.float32), "masks": masks, "wmask": bf16_words(wmask.reshape(P, 2 * P)),
            "idbf": bf16_words(np.eye(P, dtype=np.float32)), "trig": trig}


def kernel(**inputs):
    import concourse.bacc as _bacc
    from concourse.bass_utils import run_bass_kernel_spmd as _run

    nc = _bacc.Bacc("TRN2", target_bir_lowering=False, num_devices=1)
    arrays, t = {}, {}
    consts = shape_constants()
    for name in _INS + list(consts):
        a = np.ascontiguousarray(inputs[name] if name in inputs else consts[name])
        arrays[f"in_{name}"] = a
        t[name] = nc.dram_tensor(f"in_{name}", a.shape, mybir.dt.from_np(a.dtype), kind="ExternalInput").ap()
    for name, shape in _OUTS:
        t[name] = nc.dram_tensor(f"out_{name}", shape, F32, kind="ExternalOutput").ap()
    step_backbone_kernel(nc, t)
    r = _run(nc, [arrays], core_ids=[0])
    return tuple(r.results[0][f"out_{name}"] for name, _ in _OUTS)
```

```python
import math
from contextlib import ExitStack

import numpy as np
import concourse.bass as bass
from concourse import mybir

F32 = mybir.dt.float32
F32R = mybir.dt.float32r
BF16 = mybir.dt.bfloat16
U8 = mybir.dt.uint8
I32 = mybir.dt.int32
ALU = mybir.AluOpType
ACT = mybir.ActivationFunctionType
AX = mybir.AxisListType

P = 128
D = 1024
KT = D // P
NTOK = 384
TT = NTOK // P
UC = 256
EPS = 1e-6
H_A, H_B, H_C, HD = 4, 8, 8, 64
GRID_W = 64
LAM_INIT = 0.8 - 0.6 * math.exp(-0.3 * 1)
RAW = 4
LEVELS = 7

Z_F, Z_B, Q_A, Q_SWA, KV_SWA, V_A, GATE = (0, 1), (2, 3), (4, 5), (6, 7), (8,), (9, 10), (11, 12)
EVEN_COLS = [512, 768, 1024, 1280, 0, 256, 2560, 2816, 3072, 1536, 1792, 2048, 2304]
ODD_COLS = [part * 1024 + UC * j for j in range(4) for part in range(3)]
U_EVEN, U_OUT_E, U_MLP0, U_ODD, U_OUT_O, U_MLP1 = 0, 13, 17, 49, 61, 65
N_UNITS = 97
ADA_COLS = 24
SH1, SC1, G1, SH2, SC2, G2 = range(6)

STREAM = [("a", a) for a in range(6)] + [("u", 0), ("a", 6), ("a", 7), ("u", 1)]
for _u in range(2, 15):
    STREAM += [("a", 6 + _u), ("u", _u)]
STREAM += [("a", a) for a in range(21, 36)]
STREAM += [("u", _u) for _u in range(15, U_ODD + 2)]
for _i in range(12):
    STREAM += [("a", 36 + _i), ("u", U_ODD + 2 + _i)]
STREAM += [("u", _u) for _u in range(U_ODD + 14, N_UNITS)]
POS = {item: n for n, item in enumerate(STREAM)}
POOL_UNITS = [1, U_MLP0 + 1, U_ODD + 1, U_MLP1 + 1]


def high_count(u):
    return u + 1 - sum(n <= u for n in POOL_UNITS)

N_HG = 2 * (LEVELS + 1)
N_SWA = 12
EVEN_SIDE = {(6, 1): ["hg0"], (7, 0): ["hg1"], (7, 1): ["hg2"], (8, 0): ["hg3"], (8, 1): ["hg4"],
             (9, 0): ["hg5", "tq"]}
for _n in range(7):
    EVEN_SIDE[((19 + _n) // 2, (19 + _n) % 2)] = ["tk"] * (_n == 0) + [f"hg{6 + _n}", f"swa{_n}"]
EVEN_TAIL = ["swa7", "hg13", "swa8", "hg14", "swa9", "hg15", "swa10", "swa11", "swa12", "swa13", "pre", "tile"]
TAIL_ADA = 21

N_DIFF = 3 * H_C
ODD_OUT_PARTS = {20: (0, 0, 2), 21: (0, 2, 4), 22: (1, 0, 2), 23: (1, 2, 4), 24: (0, 4, 6)}
ODD_OUT_DONE = (6, 4)
ODD_HEADS = {19: (0, 1), 20: (2, 3), 22: (4, 5)}


def job(name):
    kind = name.rstrip("0123456789")
    return kind, int(name[len(kind):] or 0)


def psum_uses():
    sc, tb, ob = [], ["vecs0", "vecs1"], []
    sc.append("norm0")
    for k in range(KT):
        tb += [f"x{k}", f"ada{k}"]
        ob.append(f"ada{k}")

    def swa(s):
        if s >= 2:
            tb.extend([f"swaP{s - 2}.0", f"swaP{s - 2}.1"])
            ob.append(f"swaO{s - 2}")
        if s < N_SWA:
            sc.append(f"swa{s}")

    def even_jobs(jobs):
        for name in jobs:
            kind, i = job(name)
            if kind == "hg":
                sc.append(name)
            elif kind == "tq":
                tb.extend([f"tq{j}" for j in range(4)])
            elif kind == "tk":
                tb.append("tk")
            elif kind == "tile":
                sc.append("att8")
                tb.extend(["kf_turned", "kb_turned"])
                ob.extend(["state_f", "state_b"])
            elif kind == "swa":
                swa(i)

    for u in range(13):
        ob.append(f"ada{8 + u}")
        even_jobs(EVEN_SIDE.get((u, 0), []))
        even_jobs(EVEN_SIDE.get((u, 1), []))
        tb.append(f"ada{8 + u}")

    def tail_ada(a):
        if a > TAIL_ADA:
            tb.append(f"ada{a - 1}")
        if a < 36:
            ob.append(f"ada{a}")

    for n, name in enumerate(EVEN_TAIL):
        even_jobs([name])
        tail_ada(TAIL_ADA + n)
    for h in range(H_A):
        ob.append(f"hgO{h}")
        if h:
            tb.append(f"hgN{h - 1}")
        tail_ada(33 + h)
    tb.append("hgN3")
    sc.append("norm1")
    sc.append("norm2")

    def diff(s):
        if s >= 18 and norm_due(s):
            tb.append(f"dN{(s - 3) // 3}")
        if 2 <= s < N_DIFF + 2:
            tb.append(f"dP{s - 2}")
        if s < N_DIFF:
            sc.append(f"d{s}")
        if s >= 2 and (s - 2) % 3 == 2:
            ob.append(f"dO{(s - 2) // 3}")

    for u in range(13):
        for half in range(2):
            if half == 0 and u:
                tb.append(f"ada{35 + u}")
            if u < 12:
                tb.extend([f"dN{(s - 3) // 3}" for s in odd_slots(u, half) if norm_due(s)])
            if half == 0:
                tb.extend(odd_turns(u, 0))
                if u == 12:
                    tb.extend(odd_turns(u, 1))
            for s in odd_slots(u, half):
                diff(s)
            if u < 12:
                tb.extend(odd_turns(u, 1) if half else [f"adaM{36 + u}"])
    sc.append("norm3")
    tb.extend([f"y{k}" for k in range(KT)])
    return [{name: n for n, name in enumerate(uses)} for uses in (sc, tb, ob)]


def odd_slots(u, half):
    if u == 12:
        return list(range(18, N_DIFF + 3)) if half == 0 else []
    j = u // 3
    return [] if j == 0 else [6 * (j - 1) + 2 * (u % 3) + half]


def norm_due(s):
    return s >= 3 and s % 3 == 2


def odd_turns(u, half):
    if u == 1:
        return [f"kc{half}"]
    return [f"t{u - 2}.{half}"] if u >= 2 and (u - 2) % 3 < 2 else []


SC_USE, TB_USE, OB_USE = psum_uses()


def side_jobs(u, half):
    jobs = EVEN_SIDE.get((u, half), [])
    return [j for j in jobs if j.startswith("hg")], [j for j in jobs if not j.startswith("hg")]


def step_backbone_kernel(nc, t):
    ctx = ExitStack()
    with ctx:
        def sb(name, shape, dt=F32):
            return ctx.enter_context(nc.sbuf_tensor(name, shape, dt))

        def sem(name):
            return ctx.enter_context(nc.semaphore(name))

        xT = sb("xT", [P, KT, NTOK])
        opH = sb("opH", [P, KT, NTOK], F32R)
        opL = sb("opL", [P, KT, NTOK], F32R)
        raw = sb("raw", [P, RAW, KT, UC])
        wH = sb("wH", [P, 2, KT, UC], F32R)
        wL = sb("wL", [P, 2, KT, UC], F32R)
        nbuf = sb("nbuf", [P, 2, NTOK])
        rstd = sb("rstd", [P, NTOK])
        ident = sb("ident", [P, P])
        ones = sb("ones", [P, P])
        vecs = sb("vecs", [P, P + 26])
        cst = sb("cst", [P, KT, 32])
        mods = sb("mods", [P, 2, 48, 2])
        scale1 = sb("scale1", [P, 4, KT, 2])
        adarow = sb("adarow", [P, UC])
        small = sb("small", [P, 128])
        epsc = sb("epsc", [P, 1])
        trig = sb("trig", [P, 2, 2, HD])
        wrow = sb("wrow", [P, 4, HD])

        def arena(parts):
            held = [nc.sbuf_tensor(name, shape, dt) for name, shape, dt in parts]
            got = [h.__enter__() for h in held]
            for h in reversed(held):
                h.__exit__(None, None, None)
            return got

        xin, vrow0, vrow1 = arena([("xin", [P, TT, D], F32), ("vrow0", [P, P], F32), ("vrow1", [26, P], F32)])
        (X, hq, kk, E, vtok, att, qout, kout, vout, qT, kT, PB, PT, obuf, S0, swaK, swaV, ropeE, masks,
         wmask, idbf) = arena([
            ("X", [P, 2, 12, 129], F32),
            ("hq", [P, 12, P], F32),
            ("kk", [P, 2, 12, P], F32),
            ("E", [P, 2, 2048], F32),
            ("vtok", [P, TT, 512], F32),
            ("att", [P, 12, P], F32),
            ("qout", [P, TT, 512], F32),
            ("kout", [P, TT, P], F32),
            ("vout", [P, TT, P], F32),
            ("qT", [P, 4, NTOK], F32),
            ("kT", [P, 512], F32),
            ("PB", [P, 768], F32),
            ("PT", [P, 768], F32),
            ("obuf", [P, 4, NTOK], F32),
            ("S0", [P, 2, 4, P], F32),
            ("swaK", [P, P], F32),
            ("swaV", [P, P], F32),
            ("ropeE", [P, 2, 2, 2, HD], F32),
            ("masks", [P, 8, P], U8),
            ("wmask", [P, 2, P], BF16),
            ("idbf", [P, P], BF16)])
        hidH, hidL, relu, relu2, yout = arena([("hidH", [P, KT, NTOK], F32R), ("hidL", [P, KT, NTOK], F32R),
                                         ("relu", [P, 2, 2 * NTOK], F32), ("relu2", [P, 2, 2 * NTOK], F32),
                                         ("yout", [P, TT, D], F32)])
        (dqT, dkT, dv, dkc, dvc, draw, dsq, dout, DP, DW, DPT, doT, ropeO, lamp) = arena([
            ("dqT", [P, H_C, NTOK], F32),
            ("dkT", [P, H_C, 512], F32),
            ("dv", [P, TT, D], F32),
            ("dkc", [P, D], F32),
            ("dvc", [P, D], F32),
            ("draw", [P, 2, 768], F32),
            ("dsq", [P, 2, 768], F32),
            ("dout", [P, 2, TT, UC], F32),
            ("DP", [P, 2, 2, NTOK], F32),
            ("DW", [P, 2, NTOK], F32),
            ("DPT", [P, NTOK], F32),
            ("doT", [P, H_C, NTOK], F32),
            ("ropeO", [P, 2, 2, 2, HD], F32),
            ("lamp", [P, 4, HD], F32)])
        sb("arena_end", [P, 1])

        G = ctx.enter_context(nc.psum_tensor("G", [P, 2, 1024], F32))
        SC = ctx.enter_context(nc.psum_tensor("SC", [P, 1024], F32))
        TB = ctx.enter_context(nc.psum_tensor("TB", [P, 512], F32))
        OB = ctx.enter_context(nc.psum_tensor("OB", [P, 512], F32))

        normw = vecs[:, 0:32].rearrange("p (n t) -> p n t", n=4)
        bada = vecs[:, 32:128].rearrange("p (l i) -> p l i", l=2)
        c2 = vecs[:, P:P + 16].rearrange("p (c t) -> p c t", c=2)
        lbl = vecs[:, P + 16:P + 24]
        hgw = vecs[:, P + 24:P + 25]
        subw = vecs[:, P + 25:P + 26]
        lb, omlb = small[:, 0:8], small[:, 8:16]
        sgt = small[:, 16:32]
        ss, rs = small[:, 32:44], small[:, 44:56]
        sinkb = small[:, 56:64]
        mx, negm, dsink = small[:, 64:66], small[:, 66:68], small[:, 68:70]
        den = small[:, 70:72]
        ssum, esink, rden = (small[:, a:a + 4].rearrange("p (i c) -> p i c", c=2) for a in (108, 112, 116))
        tot = small[:, 78:86].rearrange("p (d h) -> p d h", d=2)
        lam2, lam = small[:, 86:88], small[:, 88:89]
        subs = small[:, 90:91]
        dssum = small[:, 100:104].rearrange("p (i c) -> p i c", c=2)
        drden = small[:, 104:108].rearrange("p (i c) -> p i c", c=2)
        adat = small[:, 96:100].rearrange("p (i c) -> p i c", c=2)

        def swa_probs(b):
            return PB[:, :].rearrange("p (a b) -> p a b", a=2) if b % 2 == 0 else nbuf[:, :, :]

        def swa_raw(u):
            return PB[:, :] if u % 2 == 0 else nbuf[:, :, :].rearrange("p a b -> p (a b)")

        def swa_sq(u):
            return PT[:, :] if u % 2 == 0 else obuf[:, 0:2, :].rearrange("p a b -> p (a b)")

        const_in, x_in, vec_in, even_in, odd_in, out_dma, kd_out = (
            sem(n) for n in ("const_in", "x_in", "vec_in", "even_in", "odd_in", "out_dma", "kd_out"))
        raw_in = [sem(f"raw_in{i}") for i in range(RAW)]
        w_high, pool_high, w_split, gemm_done = (sem(n) for n in ("w_high", "pool_high", "w_split", "gemm_done"))
        g_free = [sem(f"g_free{i}") for i in range(2)]
        sc_full, sc_free = sem("sc_full"), sem("sc_free")
        tb_full, tb_free = sem("tb_full"), sem("tb_free")
        ob_full, ob_free = sem("ob_full"), sem("ob_free")
        dve_step, act_step, pool_step = sem("dve_step"), sem("act_step"), sem("pool_step")
        ones_set, cst_zero, cexp_set, lbmax_sub, cst_set, mods_set = (
            sem(n) for n in ("ones_set", "cst_zero", "cexp_set", "lbmax_sub", "cst_set", "mods_set"))
        sq_set, sq_used, rstd_set = sem("sq_set"), sem("sq_used"), sem("rstd_set")
        scaled_set, oph_set, op_set = sem("scaled_set"), sem("oph_set"), sem("op_set")
        sig_set, f_set, logf_set, k_set, scans_done, silu_sig = (
            sem(n) for n in ("sig_set", "f_set", "logf_set", "k_set", "scans_done", "silu_sig"))
        hg_arg, hg_exp, hg_mul = sem("hg_arg"), sem("hg_exp"), sem("hg_mul")
        tile_arg, tile_exp, tile_mul, s0_set = (sem(n) for n in ("tile_arg", "tile_exp", "tile_mul", "s0_set"))
        rope_tab, ss_set, rs_set, xr_set, rope_set = (
            sem(n) for n in ("rope_tab", "ss_set", "rs_set", "xr_set", "rope_set"))
        negm_set, exp_set, p_set = sem("negm_set"), sem("exp_set"), sem("p_set")
        dnegm_set, dw_set, lamr_set, lam_exp = sem("dnegm_set"), sem("dw_set"), sem("lamr_set"), sem("lam_exp")
        ro_rstd, ro_set = sem("ro_rstd"), sem("ro_set")
        relu_sq, relu2_set, hid_set = sem("relu_sq"), sem("relu2_set"), sem("hid_set")

        block = ctx.enter_context(nc.Block())

        def unit_cols(w, col):
            return w[:, col:col + UC].rearrange("(k p) n -> p k n", p=P)

        @block.sync
        def _(sp):
            def load(src, pos, wait=None):
                if wait is not None:
                    sp.wait_ge(*wait)
                elif pos >= RAW:
                    kind, n = STREAM[pos - RAW]
                    if kind == "u":
                        sp.wait_ge(w_split, n + 1)
                    elif n < 36:
                        sp.wait_ge(ob_free, OB_USE[f"ada{n}"] + 1)
                    else:
                        sp.wait_ge(tb_free, TB_USE[f"adaM{n}"] + 1)
                sp.dma_start(raw[:, pos % RAW, :, :], src).then_inc(raw_in[pos % RAW], 16)

            def load_ada(a):
                load(unit_cols(t["w_ada"][a // ADA_COLS], (a % ADA_COLS) * UC), POS["a", a])

            def mlp_unit(layer, i, g):
                if i < 4:
                    src = t["w_mlp1"][layer][:, bass.ds(g * D + i * UC, UC)]
                else:
                    src = t["w_mlp2"][layer][bass.ds(g * D, D), (i - 4) * UC:(i - 3) * UC]
                return src.rearrange("(k p) n -> p k n", p=P)

            sp.dma_start(ident[:, :], t["ident"]).then_inc(const_in, 16)
            sp.dma_start(xin[:, 0, :], t["x_prompt"][0]).then_inc(x_in, 16)
            sp.dma_start(xin[:, 1:3, :], t["x_sample"][0].rearrange("(a p) d -> p a d", p=P)).then_inc(x_in, 16)
            for part, src in ((vrow0[0:32, :], t["norm_w"].rearrange("l n (t q) -> (l n t) q", q=P)),
                              (vrow0[32:P, :], t["b_ada"].rearrange("l (i q) -> (l i) q", q=P)),
                              (vrow1[0:8, :], t["c_ctx"].rearrange("(i q) -> i q", q=P)),
                              (vrow1[8:16, :], t["c"].rearrange("o (i q) -> (o i) q", q=P)),
                              (vrow1[16:24, :], t["hgrn_lb_logits"].rearrange("o d (h q) -> (o d h) q", q=P)),
                              (vrow1[24:25, :], t["hgrn_norm_w"]),
                              (vrow1[25:26, :], t["diff_subln_w"])):
                sp.dma_start(part, src).then_inc(vec_in, 16)
            for pos, (kind, n) in enumerate(STREAM[:POS["u", U_MLP0]]):
                if kind == "a":
                    load_ada(n)
                elif n < 13:
                    load(unit_cols(t["w_in_even"][0], EVEN_COLS[n]), pos)
                else:
                    load(unit_cols(t["w_out_even"][0], (n - 13) * UC), pos)
                if (kind, n) == ("u", 1):
                    sp.dma_start(wrow[:, 0, :], t["swa_qnorm_w"].broadcast_to([P, HD])).then_inc(even_in, 16)
                    sp.dma_start(wrow[:, 1, :], t["swa_knorm_w"].broadcast_to([P, HD])).then_inc(even_in, 16)
                    sp.dma_start(wrow[:, 2, :], t["diff_qnorm_w"].broadcast_to([P, HD])).then_inc(even_in, 16)
                    sp.dma_start(wrow[:, 3, :], t["diff_knorm_w"].broadcast_to([P, HD])).then_inc(even_in, 16)
                    sp.dma_start(sinkb, t["swa_sink"].broadcast_to([P, H_B])).then_inc(even_in, 16)
                    sp.dma_start(trig[:, :, :, :], t["trig"]).then_inc(even_in, 16)
                    sp.dma_start(masks[:, :, :].rearrange("p l k -> p (l k)").bitcast(I32), t["masks"]).then_inc(even_in, 16)
                    sp.dma_start(wmask[:, :, :].rearrange("p a k -> p (a k)").bitcast(I32), t["wmask"]).then_inc(even_in, 16)
                    sp.dma_start(idbf[:, :].bitcast(I32), t["idbf"]).then_inc(even_in, 16)
                    sp.dma_start(swaK[:, :], t["cache_k_swa"][0, 0].rearrange("s n d -> s (n d)")).then_inc(even_in, 16)
                    sp.dma_start(swaV[:, :], t["cache_v_swa"][0, 0].rearrange("s n d -> s (n d)")).then_inc(even_in, 16)
                    sp.dma_start(S0[:, :, :, :], t["state_hgrn"][0, 0].rearrange("d h k v -> k d h v")).then_inc(even_in, 16)
            sp.wait_ge(ob_free, OB_USE["ada35"] + 1)
            with sp.Fori(0, 4) as g:
                for i in range(8):
                    load(mlp_unit(0, i, g), POS["u", U_MLP0] + i, (w_split, U_MLP0 + i - 3 + 8 * g))
            for pos in range(POS["u", U_ODD], POS["u", U_MLP1]):
                kind, n = STREAM[pos]
                if kind == "a":
                    load_ada(n)
                elif n < U_OUT_O:
                    load(unit_cols(t["w_in_odd"][0], ODD_COLS[n - U_ODD]), pos)
                else:
                    load(unit_cols(t["w_out_odd"][0], (n - U_OUT_O) * UC), pos)
            sp.wait_ge(tb_free, TB_USE["adaM47"] + 1)
            with sp.Fori(0, 4) as g:
                for i in range(8):
                    load(mlp_unit(1, i, g), POS["u", U_MLP1] + i, (w_split, U_MLP1 + i - 3 + 8 * g))
            for k0, k1 in ((0, 6), (6, 8)):
                sp.wait_ge(tb_free, TB_USE[f"y{k1 - 1}"] + 1)
                cols = slice(P * k0, P * k1)
                sp.dma_start(t["y_prompt"][0][:, cols], yout[:, 0, cols]).then_inc(out_dma, 16)
                sp.dma_start(t["y_sample"][0].rearrange("(a p) d -> p a d", p=P)[:, :, cols],
                             yout[:, 1:3, cols]).then_inc(out_dma, 16)
            sp.wait_ge(out_dma, 16 * 8)
            sp.wait_ge(kd_out, 16 * 4)

        @block.tensor
        def _(pe):
            def take(buf, name):
                uses, free = {"sc": (SC_USE, sc_free), "tb": (TB_USE, tb_free), "ob": (OB_USE, ob_free)}[buf]
                if uses[name]:
                    pe.wait_ge(free, uses[name])

            def turn(out, src, n=P):
                return pe.transpose(out, src, ident[0:n, 0:n])

            def gemm_half(u, half, *args, **kw):
                gemm_tiles(u, 4 * half, 4 * half + 4, *args, **kw)

            def gemm_tiles(u, n0, n1, form, moving, ready=None, order=range(KT), g=0, middle={}):
                mH, mL = moving
                s = u % 2
                if n0 == 0:
                    pe.wait_ge(w_split, u + 1 + 8 * g)
                    if u >= 2:
                        pe.wait_ge(g_free[s], u // 2 + 4 * g)
                mm = None
                for n in range(n0, n1):
                    k = order[n]
                    if ready is not None:
                        ready(n)
                    first, last = n == 0, n == KT - 1
                    passes = ((wH, mH), (wH, mL), (wL, mH))
                    if form == "fm":
                        for m in range(2):
                            for q, (w, a) in enumerate(passes):
                                mm = pe.matmul(G[:, s, 512 * m:512 * m + NTOK], w[:, s, k, P * m:P * m + P],
                                               a[:, k, :], start=first and q == 0, stop=last and q == 2)
                    else:
                        for tt in range(TT):
                            for q, (w, a) in enumerate(passes):
                                mm = pe.matmul(G[:, s, UC * tt:UC * tt + UC], a[:, k, P * tt:P * tt + P],
                                               w[:, s, k, :], start=first and q == 0 and tt != 1,
                                               stop=last and q == 2, skip_group_check=True)
                    if last:
                        mm.then_inc(gemm_done, 1)
                    if n % 4 in middle:
                        middle[n % 4]()

            def ada_mm(a):
                pos = POS["a", a]
                buf, out, done, name = ("ob", OB, ob_full, "ada") if a < 36 else ("tb", TB, tb_full, "adaM")
                pe.wait_ge(raw_in[pos % RAW], 16 * (pos // RAW + 1))
                take(buf, f"{name}{a}")
                for k in range(KT):
                    j = k % 4
                    mm = pe.matmul(out[32 * j:32 * j + 32, 0:UC], cst[:, k, :], raw[:, pos % RAW, k, :],
                                   start=k < 4, stop=k >= 4, skip_group_check=True, tile_position=(0, 32 * j))
                mm.then_inc(done, 1)

            def ada_turn(a):
                if a < 36:
                    pe.wait_ge(ob_free, OB_USE[f"ada{a}"] + 1)
                take("tb", f"ada{a}")
                for i in range(2):
                    mm = turn(TB[:, P * i:P * i + P], adarow[:, P * i:P * i + P])
                mm.then_inc(tb_full, 1)

            def norm_sum(n, k):
                if k == 0:
                    take("sc", f"norm{n}")
                pe.wait_ge(sq_set, KT * n + k + 1)
                mm = pe.matmul(SC[:, 0:NTOK], ones[:, :], nbuf[:, k % 2, :], start=k == 0, stop=k == KT - 1)
                mm.then_inc(sc_full if k == KT - 1 else sq_used, 1)

            def last_norm_sums(n):
                norm_sum(n, KT - 2)
                norm_sum(n, KT - 1)

            pe.wait_ge(vec_in, 16 * 7)
            pe.wait_ge(const_in, 16)
            turn(TB[:, 0:P], vrow0[:, :]).then_inc(tb_full, 1)
            take("tb", "vecs1")
            turn(TB[:, 0:26], vrow1[:, :], 26).then_inc(tb_full, 1)
            pe.wait_ge(x_in, 32)
            pe.wait_ge(ones_set, 1)
            for k in range(KT):
                take("tb", f"x{k}")
                for tt in range(TT):
                    mm = turn(TB[:, P * tt:P * tt + P], xin[:, tt, P * k:P * k + P])
                mm.then_inc(tb_full, 1)
                if k == 0:
                    pe.wait_ge(cst_set, 1)
                ada_mm(k)
                if k:
                    norm_sum(0, k - 1)
                ada_turn(k)
            norm_sum(0, KT - 1)

            def op_ready(n_before):
                return lambda n: pe.wait_ge(op_set, n_before + n + 1)

            def hg(i):
                grp, lev = i % 2, i // 2
                take("sc", f"hg{i}")
                pe.wait_ge(hg_mul, i + 1)
                for m in range(6):
                    q = hq[:, 6 * grp + m, :] if lev == LEVELS else E[:, grp, P * m:P * m + P]
                    mm = pe.matmul(SC[:, P * m:P * m + P], E[:, grp, 1024 + P * m:1024 + P * m + P], q,
                                   start=True, stop=True, skip_group_check=True)
                mm.then_inc(sc_full, 1)

            def keys_of(ti):
                return (0, P) if ti == 0 else (P, 512)

            def swa_turn(b, hh):
                lo, hi = keys_of(b // 4)
                take("tb", f"swaP{b}.{hh}")
                pe.wait_ge(p_set, b + 1)
                for kt in range((hi - lo) // P):
                    mm = turn(TB[:, P * kt:P * kt + P], swa_probs(b)[:, hh, P * kt:P * kt + P])
                mm.then_inc(tb_full, 1)

            def swa(s):
                if s >= 2:
                    swa_turn(s - 2, 0)
                if s < N_SWA:
                    ti, pair = s // 4, s % 4
                    lo, hi = keys_of(ti)
                    take("sc", f"swa{s}")
                    pe.wait_ge(tb_free, TB_USE["tk"] + 1)
                    for hh in range(2):
                        h = 2 * pair + hh
                        b0 = 64 * (h // 4)
                        mm = pe.matmul(SC[:, 512 * hh:512 * hh + hi - lo], qT[b0:b0 + 64, h % 4, P * ti:P * ti + P],
                                       kT[b0:b0 + 64, lo:hi], start=True, stop=ti == 0, skip_group_check=True)
                        if ti:
                            off = 512 * hh + (P if ti == 1 else 0)
                            mm = pe.matmul(SC[:, off:off + P], idbf[:, :], wmask[:, ti - 1, :], start=False,
                                           stop=True, skip_group_check=True)
                    mm.then_inc(sc_full, 1)
                if s >= 2:
                    b = s - 2
                    swa_turn(b, 1)
                    ti, pair = b // 4, b % 4
                    lo, hi = keys_of(ti)
                    take("ob", f"swaO{b}")
                    kv = HD * (2 * pair // 4)
                    vals = [vout[:, 0, kv:kv + HD]] if ti == 0 else \
                        [vout[:, 1, kv:kv + HD], vout[:, 2, kv:kv + HD], swaV[:, kv:kv + HD]]
                    for hh in range(2):
                        pe.wait_ge(tb_free, TB_USE[f"swaP{b}.{hh}"] + 1)
                        for n, v in enumerate(vals):
                            mm = pe.matmul(OB[64 * hh:64 * hh + 64, 0:P], v, PT[:, NTOK * hh + P * n:NTOK * hh + P * n + P],
                                           start=n == 0, stop=n == len(vals) - 1, skip_group_check=True)
                    mm.then_inc(ob_full, 1)

            def turn_q():
                pe.wait_ge(rope_set, 2)
                for j in range(4):
                    take("tb", f"tq{j}")
                    for tt in range(TT):
                        mm = turn(TB[:, P * tt:P * tt + P], qout[:, tt, P * j:P * j + P])
                    mm.then_inc(tb_full, 1)

            def turn_k():
                take("tb", "tk")
                pe.wait_ge(rope_set, 3)
                pe.wait_ge(even_in, 16 * 12)
                for tt in range(TT):
                    turn(TB[:, P * tt:P * tt + P], kout[:, tt, :])
                turn(TB[:, NTOK:512], swaK[:, :]).then_inc(tb_full, 1)

            Eq, Ek = E[:, 0, :], E[:, 1, :]

            def hseg(e, part, h, n):
                return e[:, 1024 * part + UC * h + P * n:1024 * part + UC * h + P * n + P]

            def tile():
                take("sc", "att8")
                pe.wait_ge(tile_mul, 1)
                for h in range(H_A):
                    pe.matmul(SC[:, UC * h:UC * h + P], hseg(Ek, 1, h, 1), hseg(Eq, 1, h, 0),
                              start=True, stop=True, skip_group_check=True)
                    mm = pe.matmul(SC[:, UC * h + P:UC * h + UC], hseg(Ek, 0, h, 1), hseg(Eq, 0, h, 1),
                                   start=True, stop=True, skip_group_check=True)
                mm.then_inc(sc_full, 1)
                for d, name in enumerate(("kf_turned", "kb_turned")):
                    take("tb", name)
                    for h in range(H_A):
                        mm = turn(TB[:, P * h:P * h + P], hseg(Ek, d, h, 0))
                    mm.then_inc(tb_full, 1)
                for d, name in enumerate(("state_f", "state_b")):
                    take("ob", name)
                    pe.wait_ge(tb_free, TB_USE[("kf_turned", "kb_turned")[d]] + 1)
                    for h in range(H_A):
                        mm = pe.matmul(OB[:, P * h:P * h + P], kk[:, 1, 4 * d + h, :], vtok[:, 0, P * h:P * h + P],
                                       start=True, stop=True, skip_group_check=True)
                    mm.then_inc(ob_full, 1)

            def even_jobs(jobs):
                for name in jobs:
                    kind, i = job(name)
                    if kind == "hg":
                        hg(i)
                    elif kind == "swa":
                        swa(i)
                    elif kind == "tq":
                        turn_q()
                    elif kind == "tk":
                        turn_k()
                    elif kind == "tile":
                        tile()

            for u in range(13):
                form = "tok" if u in Q_SWA + KV_SWA + V_A else "fm"
                for half in range(2):
                    steps, others = side_jobs(u, half)
                    gemm_half(u, half, form, (opH, opL), op_ready(0) if u == 0 else None,
                              middle={2: lambda: even_jobs(steps)})
                    if half == 0:
                        ada_mm(8 + u)
                    even_jobs(others)
                ada_turn(8 + u)

            def tail_ada(a):
                if a > TAIL_ADA:
                    ada_turn(a - 1)
                if a < 36:
                    ada_mm(a)

            SWA_FIRST = [4, 5, 6, 7, 0, 1, 2, 3]

            def out_tiles(u, n0, n1):
                gemm_tiles(u, n0, n1, "fm", (opH, opL), op_ready(KT) if u == 13 else None, SWA_FIRST)

            def out_half(u, half):
                out_tiles(u, 4 * half, 4 * half + 4)

            for n, name in enumerate(EVEN_TAIL):
                even_jobs([name])
                tail_ada(TAIL_ADA + n)
                if name == "pre":
                    out_half(13, 0)

            pe.wait_ge(sc_free, SC_USE["att8"] + 1)
            pe.wait_ge(s0_set, 1)

            def v_of(tt, h):
                return vtok[:, tt, P * h:P * h + P]

            def hg_norm(h):
                take("tb", f"hgN{h}")
                pe.wait_ge(ob_free, OB_USE[f"hgO{h}"] + 1)
                pe.matmul(TB[:, 0:NTOK], ones[:, :], nbuf[:, h % 2, :], start=True, stop=True).then_inc(tb_full, 1)

            S0s = X[:, 0, 0:8, 0:P]

            for h in range(H_A):
                take("ob", f"hgO{h}")
                sums = [[(v_of(0, h), att[:, 3 * h, :])],
                        [(v_of(1, h), att[:, 3 * h + 1, :]), (v_of(2, h), kk[:, 0, 2 * h, :]),
                         (S0[:, 0, h, :], hseg(Eq, 0, h, 0)), (S0s[:, 4 + h, :], hseg(Eq, 1, h, 0))],
                        [(v_of(2, h), att[:, 3 * h + 2, :]), (v_of(1, h), kk[:, 0, 2 * h + 1, :]),
                         (S0s[:, h, :], hseg(Eq, 0, h, 1)), (S0[:, 1, h, :], hseg(Eq, 1, h, 1))]]
                for tt, terms in enumerate(sums):
                    for n, (w, a) in enumerate(terms):
                        mm = pe.matmul(OB[:, P * tt:P * tt + P], w, a, start=n == 0, stop=n == len(terms) - 1,
                                       skip_group_check=True)
                mm.then_inc(ob_full, 1)
                if h:
                    hg_norm(h - 1)
                out_tiles(14, h, h + 1)
                tail_ada(33 + h)
            hg_norm(H_A - 1)
            for u in range(13, 17):
                for half in range(2):
                    if half == 1 or u > 14:
                        out_half(u, half)
                    if half == 0 and u > 13:
                        norm_sum(1, 2 * (u - 14))
                        norm_sum(1, 2 * (u - 14) + 1)
            last_norm_sums(1)

            def mlp_group(base, g, n_op, finish=None):
                for i in range(8):
                    ready = None
                    if i == 0:
                        ready = op_ready(n_op)
                    if i == 4:
                        done = 16 if base == U_MLP1 else 0
                        ready = lambda n: pe.wait_ge(hid_set, done + 4 * g + n // 2 + 1) if n % 2 == 0 else None
                    for half in range(2):
                        gemm_half(base + i, half, "fm", (opH, opL) if i < 4 else (hidH, hidL), ready, g=g)
                        if finish is not None and i > 4:
                            finish(2 * (i - 5) + half)

            with pe.Fori(0, 3) as g:
                mlp_group(U_MLP0, g, 2 * KT)
            mlp_group(U_MLP0, 3, 2 * KT, lambda k: norm_sum(2, k))
            last_norm_sums(2)

            def diff_norm(s):
                if norm_due(s):
                    h = (s - 3) // 3
                    take("tb", f"dN{h}")
                    pe.wait_ge(ob_free, OB_USE[f"dO{h}"] + 1)
                    pe.matmul(TB[:, 0:NTOK], ones[:, :], nbuf[:, h % 2, :], start=True,
                              stop=True).then_inc(tb_full, 1)

            def diff(s):
                if s >= 18:
                    diff_norm(s)
                if 2 <= s < N_DIFF + 2:
                    b = s - 2
                    lo, hi = keys_of(b % 3)
                    take("tb", f"dP{b}")
                    pe.wait_ge(dw_set, b + 1)
                    for kt in range((hi - lo) // P):
                        mm = turn(TB[:, P * kt:P * kt + P], DW[:, b % 2, P * kt:P * kt + P])
                    mm.then_inc(tb_full, 1)
                if s < N_DIFF:
                    h, ti = s // 3, s % 3
                    lo, hi = keys_of(ti)
                    take("sc", f"d{s}")
                    pe.wait_ge(tb_free, TB_USE[f"t{3 * (h // 2) + 1}.{h % 2}"] + 1)
                    for c in range(2):
                        mm = pe.matmul(SC[:, 512 * c:512 * c + hi - lo], dqT[64 * c:64 * c + 64, h, P * ti:P * ti + P],
                                       dkT[64 * c:64 * c + 64, h, lo:hi], start=True, stop=True)
                    mm.then_inc(sc_full, 1)
                if 2 <= s < N_DIFF + 2:
                    b = s - 2
                    h, ti = b // 3, b % 3
                    if ti == 0:
                        take("ob", f"dO{h}")
                        pe.wait_ge(g_free[(U_ODD + 3 * (h // 2) + 2) % 2], (U_ODD + 3 * (h // 2) + 2) // 2 + 1)
                    pe.wait_ge(tb_free, TB_USE[f"dP{b}"] + 1)
                    vals = [dv[:, 0, P * h:P * h + P]] if ti == 0 else \
                        [dv[:, 1, P * h:P * h + P], dv[:, 2, P * h:P * h + P], dvc[:, P * h:P * h + P]]
                    for n, v in enumerate(vals):
                        mm = pe.matmul(OB[:, P * ti:P * ti + P], v, DPT[:, P * n:P * n + P], start=n == 0,
                                       stop=n == len(vals) - 1, skip_group_check=True)
                    if ti == 2:
                        mm.then_inc(ob_full, 1)

            def turns(u, half):
                for name in odd_turns(u, half):
                    take("tb", name)
                    if name.startswith("kc"):
                        pe.wait_ge(odd_in, 16 * 3)
                        for h in range(4):
                            c = D // 2 * int(name[2]) + P * h
                            mm = turn(TB[:, P * h:P * h + P], dkc[:, c:c + P])
                    else:
                        n = half
                        pe.wait_ge(rope_set, 3 + 2 * ((u - 2) // 3) + (u - 2) % 3 + 1)
                        for tt in range(TT):
                            mm = turn(TB[:, P * tt:P * tt + P], dout[:, (u - 2) % 3, tt, P * n:P * n + P])
                    mm.then_inc(tb_full, 1)

            for u in range(12):
                for half in range(2):
                    middle = {}
                    if u and half == 0:
                        middle[1] = lambda: ada_turn(35 + u)
                    if odd_slots(u, half):
                        middle[2] = lambda: diff_norm(odd_slots(u, half)[0])
                    gemm_half(U_ODD + u, half, "tok", (opH, opL), op_ready(3 * KT) if u == 0 else None,
                              middle=middle)
                    if half == 0:
                        turns(u, 0)
                    for s in odd_slots(u, half):
                        diff(s)
                    if half == 0:
                        ada_mm(36 + u)
                    else:
                        turns(u, 1)
            ada_turn(47)
            turns(12, 0)
            turns(12, 1)
            for s in odd_slots(12, 0):
                diff(s)
                if s in ODD_OUT_PARTS:
                    u, n0, n1 = ODD_OUT_PARTS[s]
                    gemm_tiles(U_OUT_O + u, n0, n1, "fm", (opH, opL), op_ready(4 * KT))
            for u in range(2):
                gemm_tiles(U_OUT_O + u, ODD_OUT_DONE[u], KT, "fm", (opH, opL), op_ready(4 * KT))
            norm_sum(3, 0)
            norm_sum(3, 1)
            for u in range(2, 4):
                for half in range(2):
                    gemm_half(U_OUT_O + u, half, "fm", (opH, opL))
                    if half == 0:
                        norm_sum(3, 2 * u - 2)
                        norm_sum(3, 2 * u - 1)
            last_norm_sums(3)
            with pe.Fori(0, 3) as g:
                mlp_group(U_MLP1, g, 5 * KT)

            def turn_y(k):
                u = N_UNITS - 4 + k // 2
                take("tb", f"y{k}")
                pe.wait_ge(g_free[u % 2], u // 2 + 1)
                for tt in range(TT):
                    mm = turn(TB[:, P * tt:P * tt + P], xT[:, k, P * tt:P * tt + P])
                mm.then_inc(tb_full, 1)

            mlp_group(U_MLP1, 3, 5 * KT, turn_y)
            turn_y(KT - 2)
            turn_y(KT - 1)

        @block.scalar
        def _(act):
            steps = [0]

            def settle(ins):
                steps[0] += 1
                ins.then_inc(act_step, 1)
                act.wait_ge(act_step, steps[0])

            def full(buf, name):
                uses, filled = {"sc": (SC_USE, sc_full), "tb": (TB_USE, tb_full), "ob": (OB_USE, ob_full)}[buf]
                act.wait_ge(filled, uses[name] + 1)

            def unit_out(u, n_cols):
                act.wait_ge(gemm_done, u + 1)
                g = G[:, u % 2, :]
                return g.rearrange("p (m n) -> p m n", m=2)[:, :, 0:NTOK] if n_cols == "fm" else g[:, 0:3 * UC]

            def split_high(u, pos, g=0):
                act.wait_ge(raw_in[pos % RAW], 16 * (pos // RAW + 1) + 16 * (8 // RAW) * g)
                if u >= 2:
                    act.wait_ge(gemm_done, u - 1 + 8 * g)
                act.activation(wH[:, u % 2, :, :], raw[:, pos % RAW, :, :], ACT.Copy).then_inc(w_high, 1)

            def split(u):
                if u < N_UNITS:
                    split_high(u, POS["u", u])

            def ada_copy(a):
                if a < 36:
                    full("ob", f"ada{a}")
                    act.activation(adarow[:, :], OB[:, 0:UC], ACT.Copy).then_inc(ob_free, 1)
                else:
                    full("tb", f"adaM{a}")
                    act.activation(adarow[:, :], TB[:, 0:UC], ACT.Copy).then_inc(tb_free, 1)

            def square(n, k):
                if k >= 2:
                    act.wait_ge(sq_used, (KT - 1) * n + k - 1)
                act.activation(nbuf[:, k % 2, :], xT[:, k, :], ACT.Square).then_inc(sq_set, 1)

            def squares(n, u, tile0):
                act.wait_ge(g_free[u % 2], u // 2 + 1)
                square(n, tile0)
                square(n, tile0 + 1)

            def norm_rstd(n):
                full("sc", f"norm{n}")
                act.activation(rstd[:, :], SC[:, 0:NTOK], ACT.Ln, bias=epsc[:, :], scale=1.0 / D).then_inc(sc_free, 1)
                act.wait_ge(sc_free, SC_USE[f"norm{n}"] + 1)
                act.activation(rstd[:, :], rstd[:, :], ACT.Exp, scale=-0.5).then_inc(rstd_set, 1)

            def shift(n):
                part = SH1 if n % 2 == 0 else SH2
                for k in range(KT):
                    act.wait_ge(scaled_set, KT * n + k + 1)
                    for c, (a, b) in enumerate(((0, P), (P, NTOK))):
                        ins = act.activation(opH[:, k, a:b], nbuf[:, k % 2, a:b], ACT.Identity,
                                             bias=mods[:, n // 2, KT * part + k, c:c + 1])
                    ins.then_inc(oph_set, 1)

            act.preload_act_table_set("natural_log_exp_and_others")
            full("tb", "vecs0")
            act.activation(vecs[:, 0:P], TB[:, 0:P], ACT.Copy).then_inc(tb_free, 1)
            full("tb", "vecs1")
            act.activation(vecs[:, P:P + 26], TB[:, 0:26], ACT.Copy).then_inc(tb_free, 1)
            act.wait_ge(tb_free, 2)
            act.activation(sgt, vecs[:, P:P + 16], ACT.Exp, scale=-1.0).then_inc(cexp_set, 1)
            act.wait_ge(lbmax_sub, 1)
            act.activation(lb, lb, ACT.Exp).then_inc(cexp_set, 1)
            act.wait_ge(ones_set, 1)
            for k in range(KT):
                full("tb", f"x{k}")
                act.activation(xT[:, k, :], TB[:, 0:NTOK], ACT.Copy).then_inc(tb_free, 1)
                act.wait_ge(tb_free, TB_USE[f"x{k}"] + 1)
                square(0, k)
                if k == 6:
                    split(0)
                ada_copy(k)
            norm_rstd(0)
            shift(0)

            def gates(u):
                d, i = u // 2, u % 2
                if u >= 2:
                    act.wait_ge(scans_done, u - 1)
                    act.wait_ge(k_set, u - 1)
                e = kk[:, d, 6 * i:6 * i + 6, :].rearrange("p a b -> p (a b)")
                act.activation(e.rearrange("p (m n) -> p m n", m=2), unit_out(u, "fm"), ACT.Exp,
                               scale=-1.0).then_inc(g_free[u % 2], 1)
                act.wait_ge(g_free[u % 2], u // 2 + 1)
                settle(act.activation(e, e, ACT.Ln, bias=ones[:, 0:1]))
                act.activation(E[:, i, 0:768], e, ACT.Exp, scale=-1.0).then_inc(sig_set, 1)

            def log_gates(u):
                act.wait_ge(f_set, u + 1)
                act.activation(E[:, u % 2, 1024:1792], E[:, u % 2, 0:768], ACT.Ln).then_inc(logf_set, 1)

            def silu_part(dst, u):
                settle(act.activation(dst.rearrange("p (m n) -> p m n", m=2), unit_out(u, "fm"), ACT.Exp, scale=-1.0))
                settle(act.activation(dst, dst, ACT.Ln, bias=ones[:, 0:1]))
                act.activation(dst, dst, ACT.Exp, scale=-1.0).then_inc(silu_sig, 1)

            def qk_rs(n_ss, count):
                act.wait_ge(ss_set, n_ss)
                settle(act.activation(rs[:, 0:count], ss[:, 0:count], ACT.Ln, bias=epsc[:, :], scale=1.0 / HD))
                act.activation(rs[:, 0:count], rs[:, 0:count], ACT.Exp, scale=-0.5).then_inc(rs_set, 1)

            def hg_exps(i):
                if i // 2 < LEVELS:
                    act.wait_ge(hg_arg, i + 1)
                    e = E[:, i % 2, :].rearrange("p (a b) -> p a b", a=2)[:, :, 0:768]
                    act.activation(e, e, ACT.Exp).then_inc(hg_exp, 1)

            def swa(s):
                if s >= 2:
                    b = s - 2
                    nk = P if b // 4 == 0 else NTOK
                    for hh in range(2):
                        full("tb", f"swaP{b}.{hh}")
                        act.activation(PT[:, NTOK * hh:NTOK * hh + nk], TB[:, 0:nk], ACT.Copy).then_inc(tb_free, 1)
                    full("ob", f"swaO{b}")
                    act.activation(obuf[:, b % 4, P * (b // 4):P * (b // 4) + P], OB[:, 0:P], ACT.Copy).then_inc(ob_free, 1)
                if s < N_SWA:
                    nk = P if s // 4 == 0 else NTOK
                    act.wait_ge(negm_set, s + 1)
                    for hh in range(2):
                        ins = act.activation(swa_probs(s)[:, hh, 0:nk], SC[:, 512 * hh:512 * hh + nk], ACT.Exp,
                                             bias=negm[:, hh:hh + 1], scale=HD ** -0.5,
                                             accum_out=ssum[:, s % 2, hh:hh + 1])
                    ins.then_inc(sc_free, 1)
                    act.activation(esink[:, s % 2, :], dsink, ACT.Exp).then_inc(exp_set, 1)

            def tile_exps():
                act.wait_ge(tile_arg, 1)
                full("sc", "hg15")
                Xf = X[:, 0, :, :].rearrange("p (h s) n -> p h s n", h=H_A)
                Xb = X[:, 1, :, :].rearrange("p (h s) n -> p h s n", h=H_A)

                def part(e, n):
                    return E[:, e, 1024 * n:1024 * n + 1024].rearrange("p (h s n) -> p h s n", h=H_A, s=2)
                act.activation(part(0, 0), Xf[:, :, 1:3, 1:129], ACT.Exp).then_inc(tile_exp, 1)
                act.activation(part(0, 1), part(0, 1), ACT.Exp).then_inc(tile_exp, 1)
                act.activation(part(1, 0), part(1, 0), ACT.Exp).then_inc(tile_exp, 1)
                act.activation(part(1, 1), Xb[:, :, 0:3:2, 0:P], ACT.Exp).then_inc(tile_exp, 1)
                act.activation(tot[:, 0, :], Xf[:, :, 1, P], ACT.Exp)
                act.activation(tot[:, 1, :], Xb[:, :, 2, P], ACT.Exp).then_inc(tile_exp, 1)

            def tile():
                full("sc", "att8")
                act.activation(kk[:, 0, 0:8, :].rearrange("p a b -> p (a b)"), SC[:, :], ACT.Copy).then_inc(sc_free, 1)
                for d, name in enumerate(("kf_turned", "kb_turned")):
                    full("tb", name)
                    act.activation(kk[:, 1, 4 * d:4 * d + 4, :].rearrange("p a b -> p (a b)"), TB[:, :],
                                   ACT.Copy).then_inc(tb_free, 1)
                for d, name in enumerate(("state_f", "state_b")):
                    full("ob", name)
                    act.activation(X[:, 1, 4 * d:4 * d + 4, 0:P], OB[:, :].rearrange("p (a b) -> p a b", a=4),
                                   ACT.Copy).then_inc(ob_free, 1)
                act.wait_ge(ob_free, OB_USE["state_b"] + 1)
                act.dma_start(t["new_state_hgrn"][0, 0].rearrange("d h k v -> k (d h) v"),
                              X[:, 1, 0:8, 0:P]).then_inc(out_dma, 16)

            def even_jobs(jobs):
                for name in jobs:
                    kind, i = job(name)
                    if kind == "hg":
                        hg_exps(i + 1)
                    elif kind == "swa":
                        swa(i)
                    elif kind == "tq":
                        for j in range(4):
                            full("tb", f"tq{j}")
                            act.activation(qT[:, j, :], TB[:, 0:NTOK], ACT.Copy).then_inc(tb_free, 1)
                    elif kind == "tk":
                        full("tb", "tk")
                        act.activation(kT[:, :], TB[:, :], ACT.Copy).then_inc(tb_free, 1)
                        act.dma_start(t["new_k_swa"][0, 0].rearrange("s n d -> s (n d)"), kout[:, 0, :]).then_inc(out_dma, 16)
                        act.dma_start(t["new_v_swa"][0, 0].rearrange("s n d -> s (n d)"), vout[:, 0, :]).then_inc(out_dma, 16)
                    elif kind == "pre":
                        tile_exps()
                    elif kind == "tile":
                        tile()

            def head_read(name, dst, sq):
                full("ob", name)
                act.activation(dst, OB[:, 0:NTOK], ACT.Copy)
                act.activation(sq, OB[:, 0:NTOK], ACT.Square).then_inc(ob_free, 1)

            def head_rstd(name, n):
                full("tb", name)
                if n:
                    act.wait_ge(ro_set, n)
                act.activation(rstd[:, :], TB[:, 0:NTOK], ACT.Ln, bias=epsc[:, :], scale=1.0 / P).then_inc(tb_free, 1)
                act.wait_ge(tb_free, TB_USE[name] + 1)
                act.activation(rstd[:, :], rstd[:, :], ACT.Exp, scale=-0.5).then_inc(ro_rstd, 1)

            for u in range(13):
                (steps0, others0), (steps1, others1) = side_jobs(u, 0), side_jobs(u, 1)
                even_jobs(steps0)
                ada_copy(8 + u)
                even_jobs(others0)
                even_jobs(steps1)
                if u in (1, 2, 3, 4):
                    log_gates(u - 1)
                if u in Z_F + Z_B:
                    gates(u)
                elif u in Q_A:
                    silu_part(hq[:, 6 * (u - 4):6 * (u - 4) + 6, :].rearrange("p a b -> p (a b)"), u)
                elif u in GATE:
                    full("tb", "tq3")
                    i = u - GATE[0]
                    silu_part(qout[:, :, :].rearrange("p a b -> p (a b)")[:, 768 * i:768 * i + 768], u)
                elif u in V_A:
                    i = u - V_A[0]
                    act.activation(vtok[:, :, UC * i:UC * i + UC], unit_out(u, "tok").rearrange("p (a b) -> p a b", a=TT),
                                   ACT.Copy).then_inc(g_free[u % 2], 1)
                elif u in Q_SWA:
                    act.activation(swa_sq(u), unit_out(u, "tok"), ACT.Square)
                    act.activation(swa_raw(u), unit_out(u, "tok"), ACT.Copy).then_inc(g_free[u % 2], 1)
                else:
                    act.wait_ge(rope_set, 1)
                    g3 = unit_out(u, "tok").rearrange("p (a b) -> p a b", a=TT)
                    act.activation(PT[:, 0:NTOK].rearrange("p (a b) -> p a b", a=TT), g3[:, :, 0:P], ACT.Square)
                    act.activation(PB[:, 0:NTOK].rearrange("p (a b) -> p a b", a=TT), g3[:, :, 0:P], ACT.Copy)
                    act.activation(vout[:, :, :], g3[:, :, P:UC], ACT.Copy).then_inc(g_free[u % 2], 1)
                even_jobs(others1)
                split(u + 2)
                if u in Q_SWA + KV_SWA:
                    qk_rs(u - Q_SWA[0] + 1, 12 if u in Q_SWA else 6)
                if u == 5:
                    hg_exps(0)
            for n, name in enumerate(EVEN_TAIL):
                even_jobs([name])
                ada_copy(TAIL_ADA + n)
                if name == "swa13":
                    act.wait_ge(ob_free, OB_USE[f"swaO{N_SWA - 1}"] + 1)
                    for k in range(4):
                        act.activation(opH[:, 4 + k, :], obuf[:, k, :], ACT.Copy).then_inc(oph_set, 1)
            for h in range(H_A + 1):
                if h < H_A:
                    head_read(f"hgO{h}", hq[:, 3 * h:3 * h + 3, :].rearrange("p a b -> p (a b)"), nbuf[:, h % 2, :])
                if h:
                    head_rstd(f"hgN{h - 1}", h - 1)
                if h < 3:
                    ada_copy(33 + h)
            for h in range(H_A):
                act.wait_ge(ro_set, h + 1)
                act.activation(opH[:, h, :], hq[:, 3 * h:3 * h + 3, :].rearrange("p a b -> p (a b)"),
                               ACT.Copy).then_inc(oph_set, 1)
            for u in range(13, 17):
                act.wait_ge(gemm_done, u + 1)
                if u < 16:
                    split(u + 2)
                squares(1, u, 2 * (u - 13))
            norm_rstd(1)
            shift(1)

            def mlp_group(base, g, pos, n_hid, last, turned_out=None, finish=None):
                for i in range(8):
                    u = base + i
                    if i == 0 and u + 1 not in POOL_UNITS:
                        split_high(u + 1, pos + 1, g)
                    if turned_out is not None and i > 4:
                        turned_out(2 * (i - 5))
                    if i < 4:
                        act.wait_ge(gemm_done, u + 1 + 8 * g)
                        if i >= 2:
                            act.wait_ge(relu2_set, n_hid + i - 1 + 4 * g)
                        r = relu[:, u % 2, :]
                        act.activation(r.rearrange("p (m n) -> p m n", m=2),
                                       G[:, u % 2, :].rearrange("p (m n) -> p m n", m=2)[:, :, 0:NTOK],
                                       ACT.Relu).then_inc(g_free[u % 2], 1)
                        act.wait_ge(g_free[u % 2], (u // 2 + 1) + 4 * g)
                        act.activation(hidH[:, 2 * i:2 * i + 2, :].rearrange("p a b -> p (a b)"), r,
                                       ACT.Square).then_inc(relu_sq, 1)
                    if i <= 5 or (i == 6 and not last):
                        split_high(u + 2, pos + i + 2, g)
                    if turned_out is not None and i > 4:
                        turned_out(2 * (i - 5) + 1)
                    if finish is not None and i >= 4:
                        finish(u, 2 * (i - 4))

            act.wait_ge(out_dma, 16 * 3)
            b0, b1 = POS["u", U_MLP0], POS["u", U_MLP1]
            mlp_group(U_MLP0, 0, b0, 0, False)
            with act.Fori(0, 2) as g:
                mlp_group(U_MLP0 + 8, g, b0 + 8, 4, False)
            mlp_group(U_MLP0 + 24, 0, b0 + 24, 12, False,
                      finish=lambda u, tile0: squares(2, u, tile0))
            norm_rstd(2)
            shift(2)

            act.wait_ge(lamr_set, 1)
            act.activation(lam2, lam2, ACT.Exp).then_inc(lam_exp, 1)

            def diff_norm(s):
                if norm_due(s):
                    h = (s - 3) // 3
                    head_rstd(f"dN{h}", H_A + h)

            def diff(s, turned_behind=lambda: None):
                if s >= 18:
                    diff_norm(s)
                if 2 <= s < N_DIFF + 2:
                    b = s - 2
                    nk = P if b % 3 == 0 else NTOK
                    full("tb", f"dP{b}")
                    act.activation(DPT[:, 0:nk], TB[:, 0:nk], ACT.Copy).then_inc(tb_free, 1)
                if s >= 2 and (s - 2) % 3 == 2:
                    h = (s - 2) // 3
                    head_read(f"dO{h}", doT[:, h, :], nbuf[:, h % 2, :])
                turned_behind()
                if s < N_DIFF:
                    nk = P if s % 3 == 0 else NTOK
                    act.wait_ge(dnegm_set, s + 1)
                    if s >= 2:
                        act.wait_ge(dw_set, s - 1)
                    for c in range(2):
                        ins = act.activation(DP[:, s % 2, c, 0:nk], SC[:, 512 * c:512 * c + nk], ACT.Exp,
                                             bias=negm[:, c:c + 1], accum_out=dssum[:, s % 2, c:c + 1])
                    ins.then_inc(sc_free, 1)

            def turned(u, half):
                for name in odd_turns(u, half):
                    full("tb", name)
                    if name.startswith("kc"):
                        n = int(name[2])
                        act.activation(dkT[:, 4 * n:4 * n + 4, NTOK:512], TB[:, :].rearrange("p (a b) -> p a b", a=4),
                                       ACT.Copy).then_inc(tb_free, 1)
                    else:
                        dst = (dqT, dkT)[(u - 2) % 3]
                        act.activation(dst[:, 2 * ((u - 2) // 3) + half, 0:NTOK], TB[:, 0:NTOK],
                                       ACT.Copy).then_inc(tb_free, 1)

            for u in range(12):
                for s in odd_slots(u, 0):
                    diff_norm(s)
                turned(u, 0)
                for s in odd_slots(u, 0):
                    diff(s)
                ada_copy(36 + u)
                for s in odd_slots(u, 1):
                    diff_norm(s)
                g = unit_out(U_ODD + u, "tok")
                part, j = u % 3, u // 3
                if part < 2:
                    if j:
                        act.wait_ge(rope_set, 3 + 2 * j + part - 1)
                    act.activation(dsq[:, part, :], g, ACT.Square)
                    act.activation(draw[:, part, :], g, ACT.Copy).then_inc(g_free[(U_ODD + u) % 2], 1)
                else:
                    act.activation(dv[:, :, UC * j:UC * j + UC], g.rearrange("p (a b) -> p a b", a=TT),
                                   ACT.Copy).then_inc(g_free[(U_ODD + u) % 2], 1)
                for s in odd_slots(u, 1):
                    diff(s, lambda: turned(u, 1))
                if not odd_slots(u, 1):
                    turned(u, 1)
                split(U_ODD + u + 2)
                if part < 2:
                    qk_rs(3 + 2 * j + part + 1, 12)
            turned(12, 0)
            turned(12, 1)
            act.wait_ge(g_free[(U_ODD + 11) % 2], (U_ODD + 11) // 2 + 1)
            act.dma_start(t["new_v_diff"][0, 0].rearrange("s h e -> s (h e)"), dv[:, 0, :]).then_inc(out_dma, 16)
            def head_high(h):
                act.wait_ge(ro_set, H_A + h + 1)
                act.activation(opH[:, h, :], doT[:, h, :], ACT.Copy).then_inc(oph_set, 1)

            for s in odd_slots(12, 0):
                for h in ODD_HEADS.get(s, ()):
                    head_high(h)
                diff(s)
            for h in range(6, H_C):
                head_high(h)
            for u in range(4):
                act.wait_ge(gemm_done, U_OUT_O + u + 1)
                if u < 3:
                    split(U_OUT_O + u + 2)
                squares(3, U_OUT_O + u, 2 * u)
            norm_rstd(3)
            shift(3)
            act.wait_ge(out_dma, 16 * 4)
            act.wait_ge(kd_out, 16 * 4)
            mlp_group(U_MLP1, 0, b1, 16, False)
            with act.Fori(0, 2) as g:
                mlp_group(U_MLP1 + 8, g, b1 + 8, 20, False)

            def copy_y(k):
                full("tb", f"y{k}")
                act.activation(yout[:, :, P * k:P * k + P], TB[:, 0:NTOK].rearrange("p (a b) -> p a b", a=TT),
                               ACT.Copy).then_inc(tb_free, 1)

            mlp_group(U_MLP1 + 24, 0, b1 + 24, 28, True, turned_out=copy_y)
            copy_y(KT - 2)
            copy_y(KT - 1)

        @block.vector
        def _(dve):
            steps = [0]

            def settle(ins):
                steps[0] += 1
                ins.then_inc(dve_step, 1)
                dve.wait_ge(dve_step, steps[0])

            def full(buf, name):
                uses, filled = {"sc": (SC_USE, sc_full), "tb": (TB_USE, tb_full)}[buf]
                dve.wait_ge(filled, uses[name] + 1)

            def split_low(u, g=0, pos=None):
                pos = POS["u", u] if pos is None else pos
                dve.wait_ge(w_high, high_count(u) + 8 * g)
                if u - 1 in POOL_UNITS:
                    dve.wait_ge(w_split, u)
                dve.tensor_tensor(wL[:, u % 2, :, :], raw[:, pos % RAW, :, :], wH[:, u % 2, :, :].bitcast(F32),
                                  ALU.subtract).then_inc(w_split, 1)

            def ada(a):
                layer, j = a // ADA_COLS, 2 * (a % ADA_COLS)
                full("tb", f"ada{a}")
                if a:
                    dve.wait_ge(mods_set, a)
                src = TB[:, 0:UC].rearrange("p (i g c) -> p i c g", i=2, g=4)[:, :, 0:2, :]
                dve.tensor_reduce(adat, src, AX.X, ALU.add).then_inc(tb_free, 1)
                dve.wait_ge(tb_free, TB_USE[f"ada{a}"] + 1)
                b = bada[:, layer, j:j + 2].rearrange("p (i o) -> p i o", o=1).broadcast_to([P, 2, 2])
                dve.tensor_tensor(mods[:, layer, j:j + 2, :], adat, b, ALU.add).then_inc(mods_set, 1)

            def scales(n, n_mods):
                dve.wait_ge(mods_set, n_mods)
                part = SC1 if n % 2 == 0 else SC2
                sc = mods[:, n // 2, KT * part:KT * part + KT, :]
                w = normw[:, n, :].rearrange("p (t o) -> p t o", o=1).broadcast_to([P, KT, 2])
                settle(dve.scalar_tensor_tensor(scale1[:, n, :, :], sc, 1.0, w, ALU.add, ALU.mult))

            def modulate(n, n_op):
                part = SH1 if n % 2 == 0 else SH2
                spans = ((0, P), (P, NTOK))
                dve.wait_ge(rstd_set, n + 1)
                for k in range(KT + 1):
                    if k < KT:
                        if k >= 2:
                            dve.wait_ge(op_set, n_op + k - 1)
                        for c, (a, b) in enumerate(spans):
                            ins = dve.scalar_tensor_tensor(nbuf[:, k % 2, a:b], xT[:, k, a:b],
                                                           scale1[:, n, k, c:c + 1], rstd[:, a:b], ALU.mult, ALU.mult)
                        ins.then_inc(scaled_set, 1)
                    if k:
                        q = k - 1
                        dve.wait_ge(oph_set, n_op + q + 1)
                        dve.wait_ge(scaled_set, KT * n + q + 1)
                        for c, (a, b) in enumerate(spans):
                            ins = dve.scalar_tensor_tensor(opL[:, q, a:b], nbuf[:, q % 2, a:b],
                                                           mods[:, n // 2, KT * part + q, c:c + 1],
                                                           opH[:, q, a:b].bitcast(F32), ALU.add, ALU.subtract)
                        ins.then_inc(op_set, 1)

            def residual(u, gate, layer, tile0, g=0):
                dve.wait_ge(gemm_done, u + 1 + 8 * g)
                for m in range(2):
                    k = tile0 + m
                    for c, (a, b) in enumerate(((0, P), (P, NTOK))):
                        ins = dve.scalar_tensor_tensor(xT[:, k, a:b], G[:, u % 2, 512 * m + a:512 * m + b],
                                                       mods[:, layer, KT * gate + k, c:c + 1], xT[:, k, a:b],
                                                       ALU.mult, ALU.add)
                ins.then_inc(g_free[u % 2], 1)

            dve.wait_ge(cexp_set, 1)
            settle(dve.tensor_scalar(sgt, sgt, 1.0, None, ALU.add))
            settle(dve.reciprocal(sgt, sgt))
            dve.wait_ge(cst_zero, 1)
            dve.tensor_tensor(cst[:, :, 0:2].rearrange("p t c -> p c t"), c2, sgt.rearrange("p (c t) -> p c t", c=2),
                              ALU.mult).then_inc(cst_set, 1)
            dve.tensor_tensor(lb, lbl, lbl, ALU.subtract).then_inc(lbmax_sub, 1)
            dve.wait_ge(cexp_set, 2)
            settle(dve.reciprocal(omlb, lb))
            settle(dve.tensor_tensor(omlb, lb, omlb, ALU.mult))
            settle(dve.tensor_tensor(lb, omlb, omlb, ALU.subtract))
            settle(dve.tensor_scalar(omlb, lb, -1.0, 1.0, ALU.mult, ALU.add))
            dve.tensor_scalar(subs, subw, 1.0 - LAM_INIT, None, ALU.mult)
            for a in range(8):
                if a == 6:
                    split_low(0)
                ada(a)
            scales(0, 8)
            modulate(0, 0)

            def forget(u):
                d, i = u // 2, u % 2
                dve.wait_ge(sig_set, u + 1)
                for m in range(2):
                    h = 4 * d + 2 * i + m
                    s = E[:, i, NTOK * m:NTOK * m + NTOK]
                    ins = dve.tensor_scalar(s, s, omlb[:, h:h + 1], lb[:, h:h + 1], ALU.mult, ALU.add)
                ins.then_inc(f_set, 1)

            def scans(u):
                d, i = u // 2, u % 2
                dve.wait_ge(logf_set, u + 1)
                for m in range(6):
                    ins = dve.tensor_tensor_scan(X[:, d, 6 * i + m, 1:129], ones[:, :],
                                                 E[:, i, 1024 + P * m:1024 + P * m + P], 0.0, ALU.mult, ALU.add)
                ins.then_inc(scans_done, 1)

            def silu_mul(dst, u, n, scale):
                dve.wait_ge(silu_sig, n)
                g = G[:, u % 2, :].rearrange("p (m n) -> p m n", m=2)[:, :, 0:NTOK]
                d = dst.rearrange("p (m n) -> p m n", m=2)
                dve.scalar_tensor_tensor(d, g, scale, d, ALU.mult, ALU.mult).then_inc(g_free[u % 2], 1)

            def qk_norm(sq, u, count):
                dve.wait_ge(g_free[u % 2], u // 2 + 1)
                dve.tensor_reduce(ss[:, 0:count], sq.rearrange("p (a b) -> p a b", b=HD), AX.X, ALU.add).then_inc(ss_set, 1)

            def qk_scale(raw3, n, count):
                dve.wait_ge(rs_set, n)
                x3 = raw3.rearrange("p (a b) -> p a b", b=HD)
                dve.tensor_tensor(x3, x3, rs[:, 0:count].rearrange("p (a o) -> p a o", o=1).broadcast_to([P, count, HD]),
                                  ALU.mult).then_inc(xr_set, 1)

            def hg_muls(i):
                grp, lev = i % 2, i // 2
                if i >= N_HG:
                    return
                if i == 0:
                    dve.wait_ge(k_set, 4)
                if lev == LEVELS:
                    full("sc", f"hg{i - 2}")
                    dve.tensor_tensor(E[:, grp, 1024:1792], kk[:, 0, 6 * grp:6 * grp + 6, :].rearrange("p a b -> p (a b)"),
                                      kk[:, 1, 6 * grp:6 * grp + 6, :].rearrange("p a b -> p (a b)"),
                                      ALU.add).then_inc(hg_mul, 1)
                    return
                dve.wait_ge(hg_exp, i + 1)
                hf = 2 ** lev
                q = E[:, grp, 0:768]
                dve.tensor_tensor(q, q, hq[:, 6 * grp:6 * grp + 6, :].rearrange("p a b -> p (a b)"), ALU.mult)
                ek = E[:, grp, 1024:1792].rearrange("p (c h j) -> p c h j", h=2, j=hf)
                for d in range(2):
                    src = kk[:, d, 6 * grp:6 * grp + 6, :].rearrange("p a (c h j) -> p (a c) h j", h=2, j=hf)
                    ins = dve.tensor_tensor(ek[:, :, d, :], ek[:, :, d, :], src[:, :, d, :], ALU.mult)
                ins.then_inc(hg_mul, 1)

            def hg_pick(i):
                grp, lev = i % 2, i // 2
                full("sc", f"hg{i}")
                dve.copy_predicated(att[:, 6 * grp:6 * grp + 6, :],
                                    masks[:, lev:lev + 1, :].broadcast_to([P, 6, P]),
                                    SC[:, 0:768].rearrange("p (a b) -> p a b", a=6)).then_inc(sc_free, 1)

            def swa(s):
                if 1 <= s < N_SWA + 1:
                    b = s - 1
                    nk = P if b // 4 == 0 else NTOK
                    dve.wait_ge(exp_set, s)
                    if b >= 2:
                        dve.wait_ge(tb_full, TB_USE[f"swaP{b - 2}.1"] + 1)
                    settle(dve.tensor_tensor(den, ssum[:, b % 2, :], esink[:, b % 2, :], ALU.add))
                    settle(dve.reciprocal(rden[:, b % 2, :], den))
                    for hh in range(2):
                        p = swa_probs(b)[:, hh, 0:nk]
                        ins = dve.tensor_scalar(p, p, rden[:, b % 2, hh:hh + 1], None, ALU.mult)
                    ins.then_inc(p_set, 1)
                if s < N_SWA:
                    ti, pair = s // 4, s % 4
                    nk = P if ti == 0 else NTOK
                    sk = sinkb[:, 2 * pair:2 * pair + 2]
                    full("sc", f"swa{s}")
                    settle(dve.tensor_reduce(mx, SC[:, :].rearrange("p (a b) -> p a b", a=2)[:, :, 0:nk], AX.X, ALU.max))
                    settle(dve.scalar_tensor_tensor(mx, mx, HD ** -0.5, sk, ALU.mult, ALU.max))
                    if s:
                        dve.wait_ge(exp_set, s)
                    dve.tensor_tensor(dsink, sk, mx, ALU.subtract)
                    dve.tensor_scalar(negm, mx, -1.0, None, ALU.mult).then_inc(negm_set, 1)

            def tile():
                q4 = hq[:, :, :].rearrange("p (h s) n -> p h s n", h=H_A)
                kf = kk[:, 0, :, :].rearrange("p (h s) n -> p h s n", h=H_A)
                kb = kk[:, 1, :, :].rearrange("p (h s) n -> p h s n", h=H_A)
                for e, n, src in ((0, 0, q4[:, :, 1:3, :]), (0, 1, q4[:, :, 1:3, :]),
                                  (1, 0, kf[:, :, 0:2, :]), (1, 1, kb[:, :, 0:3:2, :])):
                    dve.wait_ge(tile_exp, 2 * e + n + 1)
                    x = E[:, e, 1024 * n:1024 * n + 1024].rearrange("p (h s n) -> p h s n", h=H_A, s=2)
                    ins = dve.tensor_tensor(x, x, src, ALU.mult)
                ins.then_inc(tile_mul, 1)

            def even_jobs(jobs):
                for name in jobs:
                    kind, i = job(name)
                    if kind == "hg":
                        hg_pick(i)
                        hg_muls(i + 1)
                    elif kind == "swa":
                        swa(i)
                    elif kind == "pre":
                        tile()

            def low_part(k, src, n_oph):
                dve.wait_ge(oph_set, n_oph)
                dve.tensor_tensor(opL[:, k, :], src, opH[:, k, :].bitcast(F32), ALU.subtract).then_inc(op_set, 1)

            for u in range(13):
                (steps0, others0), (steps1, others1) = side_jobs(u, 0), side_jobs(u, 1)
                even_jobs(steps0 + others0 + steps1)
                if u in (1, 2, 3, 4):
                    scans(u - 1)
                if u in Z_F + Z_B:
                    forget(u)
                elif u in Q_A:
                    silu_mul(hq[:, 6 * (u - 4):6 * (u - 4) + 6, :].rearrange("p a b -> p (a b)"), u, u - 3,
                             P ** -0.5)
                elif u in GATE:
                    i = u - GATE[0]
                    silu_mul(qout[:, :, :].rearrange("p a b -> p (a b)")[:, 768 * i:768 * i + 768], u, 3 + i, 1.0)
                elif u in Q_SWA + KV_SWA:
                    count = 12 if u in Q_SWA else 6
                    qk_norm(swa_sq(u)[:, 0:HD * count], u, count)
                even_jobs(others1)
                ada(8 + u)
                split_low(u + 2)
                if u in Q_SWA + KV_SWA:
                    count = 12 if u in Q_SWA else 6
                    qk_scale(swa_raw(u)[:, 0:HD * count], u - 5, count)
                if u == 5:
                    hg_muls(0)
            for n, name in enumerate(EVEN_TAIL):
                even_jobs([name])
                if n:
                    ada(TAIL_ADA + n - 1)
                if name == "swa13":
                    for k in range(4):
                        low_part(4 + k, obuf[:, k, :], KT + k + 1)

            def head_scale(n, x, w, gate):
                dve.wait_ge(ro_rstd, n + 1)
                if gate is None:
                    dve.scalar_tensor_tensor(x, x, w, rstd[:, :], ALU.mult, ALU.mult).then_inc(ro_set, 1)
                else:
                    settle(dve.scalar_tensor_tensor(x, x, w, rstd[:, :], ALU.mult, ALU.mult))
                    dve.tensor_tensor(x, x, gate, ALU.mult).then_inc(ro_set, 1)

            gate_all = qout[:, :, :].rearrange("p a b -> p (a b)")
            dve.wait_ge(g_free[1], 6)
            dve.wait_ge(g_free[0], 7)
            for h in range(H_A):
                ada(32 + h)
                head_scale(h, hq[:, 3 * h:3 * h + 3, :].rearrange("p a b -> p (a b)"), hgw,
                           gate_all[:, NTOK * h:NTOK * h + NTOK])
            for h in range(H_A):
                low_part(h, hq[:, 3 * h:3 * h + 3, :].rearrange("p a b -> p (a b)"), KT + 4 + h + 1)
            for u in range(13, 17):
                dve.wait_ge(mods_set, 20)
                residual(u, G1, 0, 2 * (u - 13))
                if u < 16:
                    split_low(u + 2)
            scales(1, 20)
            modulate(1, 2 * KT)

            def mlp_group(layer, base, g, pos, n_hid, last):
                for i in range(8):
                    u = base + i
                    if i == 0 and u + 1 not in POOL_UNITS:
                        split_low(u + 1, g, pos + 1)
                    if i < 4:
                        dve.wait_ge(relu2_set, n_hid + i + 1 + 4 * g)
                        dve.wait_ge(relu_sq, n_hid + i + 1 + 4 * g)
                        dve.tensor_tensor(hidL[:, 2 * i:2 * i + 2, :].rearrange("p a b -> p (a b)"), relu2[:, u % 2, :],
                                          hidH[:, 2 * i:2 * i + 2, :].rearrange("p a b -> p (a b)").bitcast(F32),
                                          ALU.subtract).then_inc(hid_set, 1)
                    else:
                        residual(u, G2, layer, 2 * (i - 4), g)
                    if i <= 5 or (i == 6 and not last):
                        split_low(u + 2, g, pos + i + 2)

            b0, b1 = POS["u", U_MLP0], POS["u", U_MLP1]
            dve.wait_ge(mods_set, 24)
            mlp_group(0, U_MLP0, 0, b0, 0, False)
            with dve.Fori(0, 2) as g:
                mlp_group(0, U_MLP0 + 8, g, b0 + 8, 4, False)
            mlp_group(0, U_MLP0 + 24, 0, b0 + 24, 12, False)
            scales(2, 32)
            modulate(2, 3 * KT)

            dve.wait_ge(odd_in, 16 * 3)
            for n in range(2):
                settle(dve.tensor_tensor(lamp[:, 2 * n, :], lamp[:, 2 * n, :], lamp[:, 2 * n + 1, :], ALU.mult))
            dve.tensor_reduce(lam2, lamp[:, 0:4:2, :], AX.X, ALU.add).then_inc(lamr_set, 1)
            dve.wait_ge(lam_exp, 1)
            settle(dve.scalar_tensor_tensor(lam, lam2[:, 1:2], LAM_INIT, lam2[:, 0:1], ALU.subtract, ALU.subtract))

            def diff(s):
                if 1 <= s < N_DIFF + 1:
                    b = s - 1
                    nk = P if b % 3 == 0 else NTOK
                    dve.wait_ge(sc_free, SC_USE[f"d{b}"] + 1)
                    if b >= 2:
                        dve.wait_ge(tb_full, TB_USE[f"dP{b - 2}"] + 1)
                    dp, dw, r = DP[:, b % 2, :, 0:nk], DW[:, b % 2, 0:nk], drden[:, b % 2, :]
                    settle(dve.reciprocal(r, dssum[:, b % 2, :]))
                    settle(dve.tensor_scalar(dw, dp[:, 1, :], r[:, 1:2], lam, ALU.mult, ALU.mult))
                    dve.scalar_tensor_tensor(dw, dp[:, 0, :], r[:, 0:1], dw, ALU.mult,
                                             ALU.add).then_inc(dw_set, 1)
                if s < N_DIFF:
                    nk = P if s % 3 == 0 else NTOK
                    full("sc", f"d{s}")
                    dve.tensor_reduce(negm, SC[:, :].rearrange("p (a b) -> p a b", a=2)[:, :, 0:nk], AX.X, ALU.max,
                                      negate=True).then_inc(dnegm_set, 1)
                if norm_due(s):
                    h = (s - 3) // 3
                    head_scale(H_A + h, doT[:, h, :], subs, None)

            for u in range(12):
                part, j = u % 3, u // 3
                for s in odd_slots(u, 0):
                    diff(s)
                if part < 2:
                    qk_norm(dsq[:, part, :], U_ODD + u, 12)
                else:
                    dve.wait_ge(g_free[(U_ODD + u) % 2], (U_ODD + u) // 2 + 1)
                for s in odd_slots(u, 1):
                    diff(s)
                ada(36 + u)
                split_low(U_ODD + u + 2)
                if part < 2:
                    qk_scale(draw[:, part, :], 3 + 2 * j + part + 1, 12)
            for s in odd_slots(12, 0):
                for h in ODD_HEADS.get(s, ()):
                    low_part(h, doT[:, h, :], 4 * KT + h + 1)
                diff(s)
            for h in range(6, H_C):
                low_part(h, doT[:, h, :], 4 * KT + h + 1)
            for u in range(4):
                residual(U_OUT_O + u, G1, 1, 2 * u)
                if u < 3:
                    split_low(U_OUT_O + u + 2)
            scales(3, 48)
            modulate(3, 5 * KT)
            mlp_group(1, U_MLP1, 0, b1, 16, False)
            with dve.Fori(0, 2) as g:
                mlp_group(1, U_MLP1 + 8, g, b1 + 8, 20, False)
            mlp_group(1, U_MLP1 + 24, 0, b1 + 24, 28, True)

        @block.gpsimd
        def _(pool):
            steps = [0]

            def settle(ins):
                steps[0] += 1
                ins.then_inc(pool_step, 1)
                pool.wait_ge(pool_step, steps[0])

            pool.memset(epsc[:, :], EPS)
            pool.memset(ones[:, :], 1.0).then_inc(ones_set, 1)
            pool.memset(cst[:, :, :], 0.0).then_inc(cst_zero, 1)
            pool.wait_ge(even_in, 16 * 12)

            def tables(dst, w0):
                for n in range(2):
                    for cs in range(2):
                        w = wrow[:, w0 + n:w0 + n + 1, :].broadcast_to([P, 2, HD])
                        ins = pool.tensor_tensor(dst[:, n, cs, :, :], trig[:, cs, :, :], w, ALU.mult)
                return ins

            settle(pool.tensor_scalar(wrow[:, 2, :], wrow[:, 2, :], HD ** -0.5, None, ALU.mult))
            settle(tables(ropeE, 0))
            pool.wait_ge(tb_full, TB_USE[f"x{KT - 1}"] + 1)
            settle(pool.memset(X[:, :, :, 0:1], 0.0))

            def split(u):
                pos = POS["u", u]
                pool.wait_ge(raw_in[pos % RAW], 16 * (pos // RAW + 1))
                if u >= 2:
                    pool.wait_ge(gemm_done, u - 1)
                pool.tensor_scalar(wH[:, u % 2, :, :], raw[:, pos % RAW, :, :], 1.0, None, ALU.mult).then_inc(pool_high, 1)
                pool.wait_ge(pool_high, POOL_UNITS.index(u) + 1)
                pool.wait_ge(w_split, u)
                pool.tensor_tensor(wL[:, u % 2, :, :], raw[:, pos % RAW, :, :], wH[:, u % 2, :, :].bitcast(F32),
                                   ALU.subtract).then_inc(w_split, 1)

            split(1)

            def keys(u):
                d, i = u // 2, u % 2
                pool.wait_ge(f_set, u + 1)
                pool.tensor_scalar(kk[:, d, 6 * i:6 * i + 6, :].rearrange("p a b -> p (a b)"), E[:, i, 0:768], -1.0, 1.0,
                                   ALU.mult, ALU.add).then_inc(k_set, 1)

            def hg_args(i):
                grp, lev = i % 2, i // 2
                if lev >= LEVELS:
                    return
                if i == 0:
                    pool.wait_ge(scans_done, 4)
                    pool.wait_ge(k_set, 4)
                if i >= 2:
                    pool.wait_ge(sc_full, SC_USE[f"hg{i - 2}"] + 1)
                hf = 2 ** lev
                nb = P // (2 * hf)

                def halves(d, off):
                    x = X[:, d, 6 * grp:6 * grp + 6, off:off + P]
                    return x.rearrange("p a (c h j) -> p a c h j", h=2, j=hf)

                def mid(d):
                    return halves(d, 0)[:, :, :, 1, 0:1].broadcast_to([P, 6, nb, hf])

                q = E[:, grp, 0:768].rearrange("p (a c h j) -> p a c h j", a=6, h=2, j=hf)
                k = E[:, grp, 1024:1792].rearrange("p (a c h j) -> p a c h j", a=6, h=2, j=hf)
                pool.tensor_tensor(q[:, :, :, 1, :], halves(0, 1)[:, :, :, 1, :], mid(0), ALU.subtract)
                pool.tensor_tensor(k[:, :, :, 0, :], mid(0), halves(0, 1)[:, :, :, 0, :], ALU.subtract)
                pool.tensor_tensor(q[:, :, :, 0, :], mid(1), halves(1, 0)[:, :, :, 0, :], ALU.subtract)
                pool.tensor_tensor(k[:, :, :, 1, :], halves(1, 0)[:, :, :, 1, :], mid(1),
                                   ALU.subtract).then_inc(hg_arg, 1)

            def rope(x, tmp, tab, w, out, heads):
                c, s = (tab[:, n, :, :].rearrange("p t (o d) -> p t o d", o=1).broadcast_to([P, 2, heads, HD])
                        for n in range(2))
                pool.tensor_tensor(out[:, 0], x[:, 0], w.broadcast_to([P, heads, HD]), ALU.mult)
                pool.tensor_tensor(tmp, x[:, 1:3], s, ALU.mult)
                settle(pool.tensor_tensor(out[:, 1:3], x[:, 1:3], c, ALU.mult))
                for tt in range(2):
                    for o in range(2):
                        ins = pool.tensor_tensor(out[:, 1 + tt, :, o::2], out[:, 1 + tt, :, o::2],
                                                 tmp[:, tt, :, 1 - o::2], ALU.add)
                return ins

            def even_unit_rope(u):
                n = u - Q_SWA[0]
                pool.wait_ge(xr_set, n + 1)
                heads = 4 if u in Q_SWA else 2
                x = swa_raw(u)[:, 0:3 * HD * heads].rearrange("p (t h d) -> p t h d", t=TT, d=HD)
                tmp = swa_sq(u)[:, 0:2 * HD * heads].rearrange("p (t h d) -> p t h d", t=2, d=HD)
                if u in Q_SWA:
                    out = qout[:, :, :].rearrange("p t (h o d) -> p t h o d", o=2, d=HD)[:, :, :, n, :]
                else:
                    out = kout[:, :, :].rearrange("p t (h d) -> p t h d", d=HD)
                qk = 0 if u in Q_SWA else 1
                rope(x, tmp, ropeE[:, qk], wrow[:, qk:qk + 1, :], out, heads).then_inc(rope_set, 1)

            def states():
                pool.wait_ge(tile_exp, 5)
                for d in range(2):
                    w = tot[:, d, :].rearrange("p (h o) -> p h o", o=1).broadcast_to([P, H_A, P])
                    ins = pool.tensor_tensor(X[:, 0, 4 * d:4 * d + 4, 0:P], S0[:, d, :, :], w, ALU.mult)
                ins.then_inc(s0_set, 1)

            def tile_args():
                pool.wait_ge(sc_full, SC_USE["hg15"] + 1)
                Xf = X[:, 0, :, :].rearrange("p (h s) n -> p h s n", h=H_A)
                Xb = X[:, 1, :, :].rearrange("p (h s) n -> p h s n", h=H_A)
                qb = E[:, 0, 1024:2048].rearrange("p (h s n) -> p h s n", h=H_A, s=2)
                kf = E[:, 1, 0:1024].rearrange("p (h s n) -> p h s n", h=H_A, s=2)
                pool.tensor_tensor(qb, Xb[:, :, 1:3, P:P + 1].broadcast_to([P, H_A, 2, P]), Xb[:, :, 1:3, 0:P], ALU.subtract)
                pool.tensor_tensor(kf, Xf[:, :, 0:2, P:P + 1].broadcast_to([P, H_A, 2, P]), Xf[:, :, 0:2, 1:129],
                                   ALU.subtract).then_inc(tile_arg, 1)

            for u in range(4):
                keys(u)
            hg_args(0)
            hg_args(1)
            for u in range(6, 13):
                for half in range(2):
                    for name in EVEN_SIDE.get((u, half), []):
                        kind, i = job(name)
                        if kind == "hg":
                            hg_args(i + 2)
                if u in Q_SWA + KV_SWA:
                    even_unit_rope(u)
            for name in EVEN_TAIL:
                kind, i = job(name)
                if kind == "hg":
                    hg_args(i + 2)
                elif kind == "pre":
                    tile_args()
                    states()

            pool.wait_ge(op_set, 2 * KT)
            pool.wait_ge(out_dma, 16 * 3)
            pool.dma_start(dkc[:, :], t["cache_k_diff"][0, 0].rearrange("s h c d -> s (h c d)")).then_inc(odd_in, 16)
            pool.dma_start(dvc[:, :], t["cache_v_diff"][0, 0].rearrange("s h e -> s (h e)")).then_inc(odd_in, 16)
            pool.dma_start(lamp[:, :, :], t["diff_lambda_p"].rearrange("o a d -> o (a d)").broadcast_to([P, 4 * HD])
                           .rearrange("p (a d) -> p a d", a=4)).then_inc(odd_in, 16)
            tables(ropeO, 2).then_inc(rope_tab, 1)

            def relu_squares(base, g, n_hid):
                for i in range(4):
                    u = base + i
                    pool.wait_ge(g_free[u % 2], u // 2 + 1 + 4 * g)
                    if i >= 2:
                        pool.wait_ge(hid_set, n_hid + i - 1 + 4 * g)
                    pool.tensor_tensor(relu2[:, u % 2, :], relu[:, u % 2, :], relu[:, u % 2, :],
                                       ALU.mult).then_inc(relu2_set, 1)

            split(U_MLP0 + 1)
            with pool.Fori(0, 4) as g:
                relu_squares(U_MLP0, g, 0)

            split(U_ODD + 1)
            pool.wait_ge(rope_tab, 1)
            for j in range(4):
                for part in range(2):
                    pool.wait_ge(xr_set, 3 + 2 * j + part + 1)
                    if j:
                        pool.wait_ge(tb_full, TB_USE[f"t{3 * (j - 1) + part}.1"] + 1)
                    if j and part:
                        pool.wait_ge(kd_out, 16 * j)
                    x = draw[:, part, :].rearrange("p (t h d) -> p t h d", t=TT, d=HD)
                    tmp = dsq[:, part, 0:512].rearrange("p (t h d) -> p t h d", t=2, d=HD)
                    out = dout[:, part, :, :].rearrange("p t (h d) -> p t h d", d=HD)
                    rope(x, tmp, ropeO[:, part], wrow[:, 2 + part:3 + part, :], out, 4).then_inc(rope_set, 1)
                    if part:
                        pool.wait_ge(rope_set, 3 + 2 * (j + 1))
                        pool.dma_start(t["new_k_diff"][0, 0].rearrange("s h c d -> s (h c d)")[:, UC * j:UC * j + UC],
                                       dout[:, 1, 0, :]).then_inc(kd_out, 16)
            pool.wait_ge(out_dma, 16 * 4)
            pool.wait_ge(kd_out, 16 * 4)
            split(U_MLP1 + 1)
            with pool.Fori(0, 4) as g:
                relu_squares(U_MLP1, g, 16)


_INS = ["x_prompt", "x_sample", "cache_k_swa", "cache_v_swa", "state_hgrn", "cache_k_diff", "cache_v_diff",
        "c", "c_ctx", "norm_w", "w_ada", "b_ada", "w_in_even", "w_out_even", "hgrn_lb_logits", "hgrn_norm_w",
        "swa_qnorm_w", "swa_knorm_w", "swa_sink", "w_in_odd", "w_out_odd", "diff_qnorm_w", "diff_knorm_w",
        "diff_lambda_p", "diff_subln_w", "w_mlp1", "w_mlp2"]
_OUTS = [("y_prompt", (1, 128, 1024)), ("y_sample", (1, 256, 1024)), ("new_k_swa", (1, 1, 128, 2, 64)),
         ("new_v_swa", (1, 1, 128, 2, 64)), ("new_state_hgrn", (1, 1, 2, 4, 128, 128)),
         ("new_k_diff", (1, 1, 128, 8, 2, 64)), ("new_v_diff", (1, 1, 128, 8, 128))]


def bf16_words(a):
    return (a.view(np.uint32) >> 16).astype(np.uint16).view(np.int32)


def shape_constants():
    at = np.arange(P)
    masks = np.zeros((P, 8, P), np.uint8)
    for lev in range(LEVELS):
        same_block = (at[:, None] >> (lev + 1)) == (at[None, :] >> (lev + 1))
        other_half = (at[:, None] >> lev) != (at[None, :] >> lev)
        masks[:, lev, :] = same_block & other_half
    masks[:, LEVELS, :] = np.eye(P)
    masks = masks.reshape(P, 8 * P).view(np.int32)
    wmask = np.zeros((P, 2, P), np.float32)
    wmask[:, 0, :][at[None, :] > at[:, None]] = -1e30
    wmask[:, 1, :][at[None, :] < at[:, None]] = -1e30
    pos = np.arange(2 * P)
    row, col = (pos // GRID_W).astype(np.float32), (pos % GRID_W).astype(np.float32)
    half = HD // 2
    inv = (np.float32(10000.0) ** (-np.arange(0, half, 2, dtype=np.float32) / half)).astype(np.float32)
    ang = np.concatenate([row[:, None] * inv, col[:, None] * inv], -1)
    cos, sin = np.cos(ang), np.sin(ang)
    trig = np.zeros((P, 2, 2, HD), np.float32)
    for tt in range(2):
        rows = slice(P * tt, P * tt + P)
        trig[:, 0, tt, 0::2], trig[:, 0, tt, 1::2] = cos[rows], cos[rows]
        trig[:, 1, tt, 0::2], trig[:, 1, tt, 1::2] = sin[rows], -sin[rows]
    return {"ident": np.eye(P, dtype=np.float32), "masks": masks, "wmask": bf16_words(wmask.reshape(P, 2 * P)),
            "idbf": bf16_words(np.eye(P, dtype=np.float32)), "trig": trig}


def kernel(**inputs):
    import concourse.bacc as _bacc
    from concourse.bass_utils import run_bass_kernel_spmd as _run

    nc = _bacc.Bacc("TRN2", target_bir_lowering=False, num_devices=1)
    arrays, t = {}, {}
    consts = shape_constants()
    for name in _INS + list(consts):
        a = np.ascontiguousarray(inputs[name] if name in inputs else consts[name])
        arrays[f"in_{name}"] = a
        t[name] = nc.dram_tensor(f"in_{name}", a.shape, mybir.dt.from_np(a.dtype), kind="ExternalInput").ap()
    for name, shape in _OUTS:
        t[name] = nc.dram_tensor(f"out_{name}", shape, F32, kind="ExternalOutput").ap()
    step_backbone_kernel(nc, t)
    r = _run(nc, [arrays], core_ids=[0])
    return tuple(r.results[0][f"out_{name}"] for name, _ in _OUTS)
```
